# Optimizing a Trainium2 kernel written in Bass

```python
import jax, jax.numpy as jnp
from jax import lax
import numpy as np

D_MODEL = 1024
BATCH = 1
SEQ = 256
DEPTH = 2

N_HEADS_A = 8
HEAD_DIM = 64
D_ATTN = N_HEADS_A * HEAD_DIM
DILATED_BRANCHES = ((128, 1), (512, 4), (2048, 16))
MAX_WINDOW = 2048
Q_BLOCK = 128
POOL_WINDOWS = (2, 4, 8, 16)
N_POOL_GROUPS = 4
D_POOL = D_MODEL // 2
POOL_GROUP_DIM = D_POOL // N_POOL_GROUPS
D_MIX_EVEN = D_ATTN + D_POOL
D_IN_EVEN = 3 * D_ATTN + D_POOL
D_CONV = D_MODEL
CONV_WIDTH = 3
PEER_HEADS = 8
PEER_N_KEYS = 128
PEER_N_EXPERTS = PEER_N_KEYS * PEER_N_KEYS
PEER_TOPK = 16
PEER_D_KEY = 256
PEER_HALF = PEER_D_KEY // 2
TOKEN_CHUNK = 128
N_EVEN = (DEPTH + 1) // 2
N_ODD = DEPTH // 2
EPS = 1e-6

kernel_name = "hybrid_dilated_pool_conv_peer_trunk"

def rms_norm(x, g):
    x32 = x.astype(jnp.float32)
    y = x32 * lax.rsqrt(jnp.mean(x32 * x32, axis=-1, keepdims=True) + EPS)
    return (y * g.astype(jnp.float32)).astype(x.dtype)

def dilated_sliding_attention(q, k, v):
    b, s, h, hd = q.shape
    n_blocks = s // Q_BLOCK
    pad = ((0, 0), (MAX_WINDOW, 0), (0, 0), (0, 0))
    kp = jnp.pad(k, pad)
    vp = jnp.pad(v, pad)
    qi = jnp.arange(Q_BLOCK)
    scale = HEAD_DIM ** -0.5

    def block(i):
        s0 = i * Q_BLOCK
        qb = lax.dynamic_slice_in_dim(q, s0, Q_BLOCK, axis=1).astype(jnp.float32)
        outs, lses = [], []
        for window, dil in DILATED_BRANCHES:
            j = jnp.arange(window // dil + 1)
            pos = s0 + qi[:, None] - dil * j[None, :]
            idx = pos + MAX_WINDOW
            kg = kp[:, idx].astype(jnp.float32)
            vg = vp[:, idx].astype(jnp.float32)
            sc = jnp.einsum('bqhd,bqjhd->bqhj', qb, kg) * scale
            sc = jnp.where((pos >= 0)[None, :, None, :], sc, -jnp.inf)
            m = jnp.max(sc, axis=-1, keepdims=True)
            p = jnp.exp(sc - m)
            den = jnp.sum(p, axis=-1, keepdims=True)
            outs.append(jnp.einsum('bqhj,bqjhd->bqhd', p, vg) / den)
            lses.append(m[..., 0] + jnp.log(den[..., 0]))
        w = jax.nn.softmax(jnp.stack(lses, axis=-1), axis=-1)
        o = jnp.sum(w[..., None] * jnp.stack(outs, axis=3), axis=3)
        return o.astype(v.dtype)

    out = lax.map(block, jnp.arange(n_blocks))
    return out.transpose(1, 0, 2, 3, 4).reshape(b, s, h * hd)

def multiscale_pool(u, pool_w, pool_scale):
    b, s, _ = u.shape
    ug = u.reshape(b, s, N_POOL_GROUPS, POOL_GROUP_DIM)
    cs0 = jnp.pad(jnp.cumsum(ug.astype(jnp.float32), axis=1), ((0, 0), (1, 0), (0, 0), (0, 0)))
    t1 = jnp.arange(1, s + 1, dtype=jnp.float32)
    pooled = []
    for gi, w in enumerate(POOL_WINDOWS):
        cg = cs0[:, :, gi]
        upper = cg[:, 1:]
        lower = jnp.pad(cg, ((0, 0), (w - 1, 0), (0, 0)))[:, :s]
        cnt = jnp.minimum(t1, float(w))[None, :, None]
        pooled.append((upper - lower) / cnt)
    pooled = jnp.stack(pooled, axis=2)
    diff = (pooled - ug.astype(jnp.float32)).astype(u.dtype)
    y = jnp.einsum('bsgc,gcd->bsgd', diff, pool_w)
    return y.reshape(b, s, D_POOL) * pool_scale

def short_gated_conv(h, w_in, conv_w, w_out):
    s = h.shape[1]
    xin, gate_b, gate_c = jnp.split(h @ w_in, 3, axis=-1)
    u = gate_c * xin
    up = jnp.pad(u, ((0, 0), (CONV_WIDTH - 1, 0), (0, 0)))
    y = conv_w[0] * up[:, CONV_WIDTH - 1:CONV_WIDTH - 1 + s]
    for lag in range(1, CONV_WIDTH):
        y = y + conv_w[lag] * up[:, CONV_WIDTH - 1 - lag:CONV_WIDTH - 1 - lag + s]
    return (gate_b * y) @ w_out

def peer_ffn(h, w_q, key1, key2, u_tab, v_tab):
    b, s, d = h.shape
    hc = h.reshape((b * s) // TOKEN_CHUNK, TOKEN_CHUNK, d)

    def chunk(xc):
        q = (xc @ w_q).reshape(TOKEN_CHUNK, PEER_HEADS, PEER_D_KEY).astype(jnp.float32)
        s1 = jnp.einsum('thc,nc->thn', q[..., :PEER_HALF], key1.astype(jnp.float32))
        s2 = jnp.einsum('thc,nc->thn', q[..., PEER_HALF:], key2.astype(jnp.float32))
        v1, i1 = lax.top_k(s1, PEER_TOPK)
        v2, i2 = lax.top_k(s2, PEER_TOPK)
        cand = (v1[..., :, None] + v2[..., None, :]).reshape(TOKEN_CHUNK, PEER_HEADS, PEER_TOPK * PEER_TOPK)
        vs, ci = lax.top_k(cand, PEER_TOPK)
        e1 = jnp.take_along_axis(i1, ci // PEER_TOPK, axis=-1)
        e2 = jnp.take_along_axis(i2, ci % PEER_TOPK, axis=-1)
        expert = e1 * PEER_N_KEYS + e2
        g = jax.nn.softmax(vs, axis=-1)
        act = jax.nn.gelu(jnp.einsum('td,thkd->thk', xc, u_tab[expert]), approximate=False)
        return jnp.einsum('thk,thkd->td', (g * act).astype(xc.dtype), v_tab[expert])

    return lax.map(chunk, hc).reshape(b, s, d)

def setup_inputs(seed: int = 0) -> dict:
    key = jax.random.key(seed)
    ks = jax.random.split(key, 24)
    f32 = jnp.float32

    def nrm(k, shape, scale):
        return jax.random.normal(k, shape, f32) * scale

    D = D_MODEL
    return {
        "x": nrm(ks[0], (BATCH, SEQ, D), 1.0),
        "c": nrm(ks[1], (BATCH, D), 1.0),
        "ada_w": nrm(ks[2], (DEPTH, D, 6 * D), D ** -0.5),
        "ada_b": nrm(ks[3], (DEPTH, 6 * D), 0.02),
        "norm_mix_g": 1.0 + nrm(ks[4], (DEPTH, D), 0.02),
        "norm_ffn_g": 1.0 + nrm(ks[5], (DEPTH, D), 0.02),
        "ab_w_in": nrm(ks[6], (N_EVEN, D, D_IN_EVEN), D ** -0.5),
        "ab_q_gain": 1.0 + nrm(ks[7], (N_EVEN, N_HEADS_A, HEAD_DIM), 0.02),
        "ab_k_gain": 1.0 + nrm(ks[8], (N_EVEN, N_HEADS_A, HEAD_DIM), 0.02),
        "pool_w": nrm(ks[9], (N_EVEN, N_POOL_GROUPS, POOL_GROUP_DIM, POOL_GROUP_DIM), POOL_GROUP_DIM ** -0.5),
        "pool_scale": 1.0 + nrm(ks[10], (N_EVEN, D_POOL), 0.1),
        "ab_w_out": nrm(ks[11], (N_EVEN, D_MIX_EVEN, D), D_MIX_EVEN ** -0.5),
        "conv_w_in": nrm(ks[12], (N_ODD, D, 3 * D_CONV), D ** -0.5),
        "conv_w": nrm(ks[13], (N_ODD, CONV_WIDTH, D_CONV), CONV_WIDTH ** -0.5),
        "conv_w_out": nrm(ks[14], (N_ODD, D_CONV, D), D_CONV ** -0.5),
        "peer_w_q": nrm(ks[15], (DEPTH, D, PEER_HEADS * PEER_D_KEY), D ** -0.5),
        "peer_key1": nrm(ks[16], (DEPTH, PEER_N_KEYS, PEER_HALF), PEER_HALF ** -0.5),
        "peer_key2": nrm(ks[17], (DEPTH, PEER_N_KEYS, PEER_HALF), PEER_HALF ** -0.5),
        "peer_u": nrm(ks[18], (DEPTH, PEER_N_EXPERTS, D), D ** -0.5),
        "peer_v": nrm(ks[19], (DEPTH, PEER_N_EXPERTS, D), PEER_TOPK ** -0.5),
    }

def reference(x, c, ada_w, ada_b, norm_mix_g, norm_ffn_g, ab_w_in, ab_q_gain, ab_k_gain,
              pool_w, pool_scale, ab_w_out, conv_w_in, conv_w, conv_w_out,
              peer_w_q, peer_key1, peer_key2, peer_u, peer_v):
    b, s, _ = x.shape
    c_act = jax.nn.silu(c)
    for layer in range(DEPTH):
        mod = c_act @ ada_w[layer] + ada_b[layer]
        sh1, sc1, g1, sh2, sc2, g2 = [m[:, None, :] for m in jnp.split(mod, 6, axis=-1)]
        h = rms_norm(x, norm_mix_g[layer]) * (1.0 + sc1) + sh1
        if layer % 2 == 0:
            e = layer // 2
            proj = h @ ab_w_in[e]
            q, k, v, u = jnp.split(proj, [D_ATTN, 2 * D_ATTN, 3 * D_ATTN], axis=-1)
            q = rms_norm(q.reshape(b, s, N_HEADS_A, HEAD_DIM), ab_q_gain[e])
            k = rms_norm(k.reshape(b, s, N_HEADS_A, HEAD_DIM), ab_k_gain[e])
            v = v.reshape(b, s, N_HEADS_A, HEAD_DIM)
            y_attn = dilated_sliding_attention(q, k, v)
            y_pool = multiscale_pool(u, pool_w[e], pool_scale[e])
            y = jnp.concatenate([y_attn, y_pool], axis=-1) @ ab_w_out[e]
        else:
            o = layer // 2
            y = short_gated_conv(h, conv_w_in[o], conv_w[o], conv_w_out[o])
        x = x + g1 * y
        h = rms_norm(x, norm_ffn_g[layer]) * (1.0 + sc2) + sh2
        x = x + g2 * peer_ffn(h, peer_w_q[layer], peer_key1[layer], peer_key2[layer],
                              peer_u[layer], peer_v[layer])
    return x


_drawn_inputs = setup_inputs


def setup_inputs(seed=0):
    import zlib

    import numpy as np

    out = dict(_drawn_inputs(seed))
    spreads = {}
    factors = {'norm_ffn_g': 3.106, 'ab_q_gain': 8.0, 'ab_k_gain': 8.0}
    for name, (base, spread) in spreads.items():
        noise = np.random.default_rng([zlib.crc32(name.encode()), seed]).standard_normal(out[name].shape)
        drawn = base * np.exp(spread * noise) if base else spread * noise
        out[name] = __import__('jax').numpy.asarray(drawn.astype(out[name].dtype))
    for name, factor in factors.items():
        out[name] = (out[name] * factor).astype(out[name].dtype)
    return out
```

```python
from contextlib import ExitStack

import concourse.bass as bass
from concourse import mybir
from concourse.alu_op_type import AluOpType as ALU

F32 = mybir.dt.float32
I32 = mybir.dt.int32
U32 = mybir.dt.uint32
ACT = mybir.ActivationFunctionType
AX = mybir.AxisListType

P = 128
D = 1024
KC = D // P
NT = 512
LAYERS = 2
CHUNKS = 2
HEADS, HD = 8, 64
WINDOWS = (2, 4, 8, 16)
GROUPS = len(WINDOWS)
CONV = 3
PH, PK = 8, 16
NKEY = 128
EPS = 1e-6
LOWEST = -3.0e38
MASKED = -1.0e30
SLOTS = PH * PK
RING = 8
GS = 4
GG = SLOTS // GS
WR = 5

MOD_TILES = 6 * D // NT
MIX0_TILES = 4
MIX1_TILES = 6
OUT_TILES = D // NT
WQ_TILES = 2 * PH * P // NT
CONV_ORDER = (0, 4, 2, 1, 5, 3)


def mix_tiles(layer):
    return MIX1_TILES if layer else MIX0_TILES


def visit_tiles(layer):
    return mix_tiles(layer) + OUT_TILES + WQ_TILES


def mod_tile(layer, i):
    return i + (MOD_TILES + CHUNKS * visit_tiles(0) if layer else 0)


def tile(v, stage, i):
    layer, c = divmod(v, CHUNKS)
    before = (0, mix_tiles(layer), mix_tiles(layer) + OUT_TILES)[stage]
    return mod_tile(layer, MOD_TILES) + c * visit_tiles(layer) + before + i


TB0 = {"h": 0, "qk": 2, "p": 4, "o": 4 + HEADS, "f": 5 + HEADS, "wq": 7 + HEADS, "end": 7 + HEADS + WQ_TILES}
TB1 = {"h": 0, "ub": 2, "f": 6, "wq": 8, "end": 8 + WQ_TILES}


def batch(v, name, i=0):
    layer, c = divmod(v, CHUNKS)
    of = TB1 if layer else TB0
    return (CHUNKS * TB0["end"] if layer else 0) + c * of["end"] + of[name] + i


GAIN_PARTS = (1, 4)


def rows_landed(n):
    tiles = range(n % 2, n + 1, 2)
    return sum(32 if m % MOD_TILES // 2 in GAIN_PARTS else 16 for m in tiles)


def gains_until(layer, i):
    return 4 * layer + sum(m // 2 in GAIN_PARTS for m in range(i + 1))


def trunk(nc, a, out):
    source = {}
    for layer in range(LAYERS):
        for i in range(MOD_TILES):
            source[mod_tile(layer, i)] = (a["ada_w"][layer], i)
        for c in range(CHUNKS):
            v = CHUNKS * layer + c
            w_in = a["conv_w_in"][0] if layer else a["ab_w_in"][0]
            w_out = a["conv_w_out"][0] if layer else a["ab_w_out"][0]
            for i in range(mix_tiles(layer)):
                source[tile(v, 0, i)] = (w_in, CONV_ORDER[i] if layer else i)
            for i in range(OUT_TILES):
                source[tile(v, 1, i)] = (w_out, i)
            for i in range(WQ_TILES):
                source[tile(v, 2, i)] = (a["peer_w_q"][layer], i)
    TILES = len(source)

    ctx = ExitStack()
    with ctx:
        def sb(name, shape, dt=F32):
            return ctx.enter_context(nc.sbuf_tensor("t_" + name, shape, dt))

        def pb(name, shape):
            return ctx.enter_context(nc.psum_tensor("p_" + name, shape, F32))

        def sem(name):
            return ctx.enter_context(nc.semaphore("s_" + name))

        ring = sb("ring", [P, RING, 2 * D])
        wring = sb("wring", [P, WR, KC // 2, NT])
        x = sb("x", [P, CHUNKS, D])
        mod = sb("mod", [P, 7, D])
        h2 = sb("h2", [P, CHUNKS, D])
        hT = sb("hT", [P, KC, P])
        hm = sb("hm", [P, D])
        zT = hm[:, :].rearrange("p (k t) -> p k t", k=KC)
        ident = sb("ident", [P, P])
        bias = sb("bias", [P, 3 * P])
        poolm = sb("poolm", [P, 3, GROUPS, P])
        poolw = sb("poolw", [P, GROUPS, P])
        keyT = sb("keyT", [P, LAYERS, 2, P])
        cols = sb("cols", [P, KC + 3 * 4 + CONV * KC])
        cT = cols[:, 0:8]
        qgain, kgain, pscale = cols[:, 8:12], cols[:, 12:16], cols[:, 16:20]
        convw = cols[:, 20:44].rearrange("p (l k) -> p l k", l=CONV)
        iota = sb("iota", [P, PK])
        silu = sb("silu", [P, 3, KC])
        cact = hT

        keep = sb("keep", [P, 3104])
        kT = keep[:, 0:1024].rearrange("p (j t) -> p j t", j=4)
        vtok = keep[:, 1024:2048].rearrange("p (c n) -> p c n", c=CHUNKS)
        utok = keep[:, 2048:3072].rearrange("p (c n) -> p c n", c=CHUNKS)
        uT = keep[:, 0:1040].rearrange("p (k t) -> p k t", k=KC)
        bT = keep[:, 1040:2064].rearrange("p (k t) -> p k t", k=KC)
        lagT = keep[:, 2064:3088].rearrange("p (k t) -> p k t", k=KC)
        work = sb("work", [P, 3072])
        qk = work[:, 0:1024]
        otok = work[:, 0:512]
        qT = work[:, 1024:1536].rearrange("p (j t) -> p j t", j=4)
        sc = work[:, 1536:2048].rearrange("p (b t) -> p b t", b=2)
        dT = work[:, 1536:2048].rearrange("p (g t) -> p g t", g=GROUPS)
        pr = work[:, 2048:2560].rearrange("p (b t) -> p b t", b=2)
        prT = work[:, 2560:3072].rearrange("p (b k t) -> p b k t", b=2, k=2)
        xin, uhalf, bhalf = work[:, 0:512], work[:, 512:1024], work[:, 1024:1536]
        ytmp = work[:, 2048:2560]
        S = work[:, 0:2048].rearrange("p (h s n) -> p h s n", h=PH, s=2)
        qtok = work[:, 2048:2560]
        qhT = work[:, 2560:3072].rearrange("p (j t) -> p j t", j=4)
        brow = work[:, 0:1024].rearrange("p (b n) -> p b n", b=2)
        grow = work[:, 1024:2048].rearrange("p (b n) -> p b n", b=2)
        cand, cand2 = hm[:, 0:256], hm[:, 256:512]
        s2 = hm[:, 512:640]
        hot = hm[:, :]

        v16 = sb("v16", [P, PH, 2, PK])
        i16 = sb("i16", [P, PH, 2, PK], U32)
        vs = sb("vs", [P, PH, PK])
        ci = sb("ci", [P, PH, PK], U32)
        cab = work[:, 0:2 * SLOTS].bitcast(U32).rearrange("p (s j) -> p s j", s=2)
        sub = work[:, 2 * SLOTS:4 * SLOTS].rearrange("p (s j) -> p s j", s=2)
        ids = sb("ids", [P, 2, SLOTS], U32)
        gates = sb("gates", [P, 2, SLOTS])
        small = sb("small", [P, 96])
        ss, ve, rs, r2 = small[:, 0:1], small[:, 1:2], small[:, 2:3], small[:, 3:4]
        ssq, veq, rsq, r2q = small[:, 16:32], small[:, 32:48], small[:, 48:64], small[:, 64:80]
        att = sb("att", [P, 4, HEADS])
        gsum = sb("gsum", [P, 2, PH])
        dots = sb("dots", [P, 2, GS])
        gel = sb("gel", [P, 2, GS])
        coef = sb("coef", [P, 2, GS])
        diag = sb("diag", [P, 2, GS, P])
        otmp = diag[:, 0, :, :].rearrange("p s t -> p (s t)")

        acc = [pb(f"acc{i}", [P, NT]) for i in range(2)]
        pG = [pb(f"g{i}", [P, NT]) for i in range(2)]
        pT = [pb(f"t{i}", [P, NT]) for i in range(2)]
        pS = pb("s", [P, NT])
        pO = pb("o", [P, NT])
        score_bank = (pS, pG[1])

        consts = sem("consts")
        w_in = [sem(f"w_in{i}") for i in range(WR)]
        half_done = sem("half_done")

        t_done = sem("t_done")
        g_read = [sem(f"g_read{i}") for i in range(2)]
        t_copied = sem("t_copied")
        brow_in = [sem(f"brow_in{i}") for i in range(2)]
        scaled = sem("scaled")
        silu_step = sem("silu_step")
        chain = sem("chain")
        h_ready = sem("h_ready")
        qk_ready = sem("qk_ready")
        scored = sem("scored")
        maxed = sem("maxed")
        masked = sem("masked")
        expd = sem("expd")
        pv_done = sem("pv_done")
        otok_ready = sem("otok_ready")
        diff_done = sem("diff_done")
        dT_ready = sem("dT_ready")
        pooled = sem("pooled")
        zT_ready = sem("zT_ready")
        x_mixed = sem("x_mixed")
        keyed = sem("keyed")
        S_in = sem("S_in")
        shifted = sem("shifted")
        gexp = sem("gexp")
        routed = sem("routed")
        row_in = [sem(f"row_in{i}") for i in range(RING)]
        dotted = sem("dotted")
        gelued = sem("gelued")
        diag_ready = sem("diag_ready")
        summed = sem("summed")
        x_summed = sem("x_summed")
        stored = sem("stored")

        CONSTS = 16 * 8

        def pieces(v):
            if v // CHUNKS == 0:
                names = [("norm", 0)] + [("in", i) for i in range(MIX0_TILES)]
                names += [("qknorm", 0), ("pool", 0)] + [("head", i) for i in range(HEADS)] + [("attout", 0)]
            else:
                names = [("norm", 0)] + [("in", i) for i in range(MIX1_TILES)] + [("conv", 0)]
            names += [("out", i) for i in range(OUT_TILES)] + [("norm", 1)]
            names += [("wq", i) for i in range(WQ_TILES)] + [("route", i) for i in range(PH)] + [("pick", 0)]
            return [(n, v, i) for n, i in names]

        def woven(v, other):
            steps, n = [], len(other)
            for g in range(GG):
                steps.append(("gather", v, g))
                steps += other[g * n // GG:(g + 1) * n // GG]
            return steps + [("finish", v, 0)]

        mods = [[("mod", layer, i) for i in range(MOD_TILES)] for layer in range(LAYERS)]
        order = mods[0] + pieces(0) + woven(0, pieces(1)) + woven(1, mods[1] + pieces(2))
        order += woven(2, pieces(3)) + woven(3, [])

        def wait_read(engine, t):
            engine.wait_ge(g_read[t % 2], t // 2 + 1)

        block = ctx.enter_context(nc.Block())

        @block.sync
        def _(sp):
            sp.dma_start(cols[:, :], a["cols"]).then_inc(consts, 16)

            def load_weights(t):
                for half in range(2):
                    n = 2 * t + half
                    if n >= WR:
                        sp.wait_ge(half_done, n - WR + 1)
                    w, i = source[t]
                    rows = w[half * D // 2:(half + 1) * D // 2, i * NT:(i + 1) * NT]
                    sp.dma_start(wring[:, n % WR, :, :], rows.rearrange("(k p) n -> p k n", p=P))\
                        .then_inc(w_in[n % WR], 16)

            early = 2
            for t in range(early):
                load_weights(t)
            sp.dma_start(x[:, :, :], a["x"][0].rearrange("(c p) d -> p c d", p=P)).then_inc(consts, 16)
            sp.dma_start(ident[:, :], a["ident"]).then_inc(consts, 16)
            sp.dma_start(bias[:, :], a["bias"]).then_inc(consts, 16)
            sp.dma_start(poolm[:, :, :, :], a["poolm"]).then_inc(consts, 16)
            sp.dma_start(poolw[:, :, :], a["pool_w"][0].rearrange("g c d -> c g d")).then_inc(consts, 16)
            sp.dma_start(keyT[:, :, :, :], a["keyT"]).then_inc(consts, 16)
            sp.dma_start(iota[:, :], a["iota"]).then_inc(consts, 16)
            for t in range(early, TILES):
                load_weights(t)
            for c in range(CHUNKS):
                sp.wait_ge(x_summed, 2 * (CHUNKS + c + 1))
                sp.dma_start(out[0, c * P:(c + 1) * P, :], x[:, c, :]).then_inc(stored, 16)
            sp.wait_ge(stored, 16 * CHUNKS)

        @block.gpsimd
        def _(pool):
            for v in range(LAYERS * CHUNKS):
                pool.wait_ge(routed, v + 1)
                layer = v // CHUNKS
                for j in range(SLOTS):
                    n = v * SLOTS + j
                    if n >= RING:
                        pool.wait_ge(summed, n - RING + 1)
                    nc.gpsimd.indirect_dma_start(
                        out=ring[:, n % RING, :], out_offset=None, in_=a[f"uv{layer}"],
                        in_offset=bass.IndirectOffsetOnAxis(ap=ids[:, v % 2, j:j + 1], axis=0),
                    ).then_inc(row_in[n % RING], 16)

        @block.tensor
        def _(pe):
            pe.wait_ge(consts, CONSTS)

            def product(t, lhsT, first=0):
                bank = t % 2
                if t >= 2:
                    pe.wait_ge(g_read[bank], t // 2)
                for half in range(2):
                    n = 2 * t + half
                    pe.wait_ge(w_in[n % WR], 16 * (n // WR + 1))
                    for k in range(KC // 2):
                        kk = half * KC // 2 + k
                        last = nc.tensor.matmul(pG[bank][:, :], lhsT(kk), wring[:, n % WR, k, :],
                                                start=kk == 0, stop=kk == KC - 1)
                    last.then_inc(half_done, 1)

            def transposes(b, blocks):
                if b >= 2:
                    pe.wait_ge(t_copied, b - 1)
                for i, block_ in enumerate(blocks):
                    last = nc.tensor.transpose(pT[b % 2][:, i * P:(i + 1) * P], block_, ident[:, :])
                last.then_inc(t_done, 1)

            def mod_(layer, i):
                if i == 0:
                    pe.wait_ge(silu_step, 4 + layer)
                product(mod_tile(layer, i), lambda k: cact[:, k, :])

            def norm(v, which):
                c = v % CHUNKS
                pe.wait_ge(h_ready, 2 * v + which + 1)
                src = h2[:, c, :] if which else hm[:, :]
                for i in range(2):
                    transposes(batch(v, "f" if which else "h", i),
                               [src[:, (4 * i + j) * P:(4 * i + j + 1) * P] for j in range(4)])

            def in_(v, i):
                layer, c = divmod(v, CHUNKS)
                if i == 0:
                    pe.wait_ge(t_copied, batch(v, "h", 1) + 1)
                product(tile(v, 0, i), lambda k: hT[:, k, :])
                if layer and i % 3 == 2:
                    half = i // 3
                    n = 2 * c + half
                    wait_read(pe, tile(v, 0, 3 * half + 1))
                    transposes(batch(v, "ub", 2 * half), [uhalf[:, j * P:(j + 1) * P] for j in range(4)])
                    wait_read(pe, tile(v, 0, 3 * half + 2))
                    transposes(batch(v, "ub", 2 * half + 1), [bhalf[:, j * P:(j + 1) * P] for j in range(4)])

            def qknorm(v, _):
                pe.wait_ge(qk_ready, v + 1)
                for i in range(2):
                    transposes(batch(v, "qk", i), [qk[:, (4 * i + j) * P:(4 * i + j + 1) * P] for j in range(4)])

            def pool_(v, _):
                c = v % CHUNKS
                wait_read(pe, tile(v, 0, 3))
                if v:
                    pe.wait_ge(S_in, WQ_TILES * v)
                for g in range(GROUPS):
                    for s in range(c + 1):
                        which = (0 if c == 0 else 2 if s == 0 else 1)
                        last = nc.tensor.matmul(pS[:, g * P:(g + 1) * P], utok[:, s, g * P:(g + 1) * P],
                                                poolm[:, which, g, :], start=s == 0, stop=s == c)
                last.then_inc(diff_done, 1)
                pe.wait_ge(dT_ready, v + 1)
                for g in range(GROUPS):
                    last = nc.tensor.matmul(pO[:, g * P:(g + 1) * P], poolw[:, g, :], dT[:, g, :],
                                            start=True, stop=True)
                last.then_inc(pooled, 1)

            def head(v, i):
                c = v % CHUNKS
                keys = (c + 1) * P

                def scores(h):
                    n = HEADS * v + h
                    if h == 0:
                        pe.wait_ge(t_copied, batch(v, "qk", 1) + 1)
                        wait_read(pe, tile(v, 0, 3))
                        pe.wait_ge(dT_ready, v + 1)
                    elif h >= 2:
                        pe.wait_ge(maxed, n - 1)
                    if h:
                        pe.wait_ge(scored, n)
                    rows = slice(HD * (h % 2), HD * (h % 2) + HD)
                    nc.tensor.matmul(score_bank[h % 2][:, 0:keys], qT[rows, h // 2, :],
                                     kT[rows, h // 2, 0:keys], start=True, stop=True).then_inc(scored, 1)

                if i == 0:
                    scores(0)
                if i + 1 < HEADS:
                    scores(i + 1)
                n = HEADS * v + i
                pe.wait_ge(expd, n + 1)
                transposes(batch(v, "p", i), [pr[:, i % 2, k * P:(k + 1) * P] for k in range(c + 1)])
                pe.wait_ge(t_copied, batch(v, "p", i) + 1)
                if i == 0:
                    pe.wait_ge(zT_ready, v + 1)
                for k in range(c + 1):
                    last = nc.tensor.matmul(pO[:, i * HD:(i + 1) * HD], prT[:, i % 2, k, :],
                                            vtok[:, k, i * HD:(i + 1) * HD], start=k == 0, stop=k == c)
                last.then_inc(pv_done, 1)

            def attout(v, _):
                pe.wait_ge(otok_ready, v + 1)
                transposes(batch(v, "o"), [otok[:, j * P:(j + 1) * P] for j in range(4)])

            def out_(v, i):
                if i == 0:
                    pe.wait_ge(zT_ready, v + 1)
                    if v < CHUNKS:
                        pe.wait_ge(t_copied, batch(v, "o") + 1)
                product(tile(v, 1, i), lambda k: zT[:, k, :])

            def wq(v, i):
                layer = v // CHUNKS
                if i == 0:
                    pe.wait_ge(t_copied, batch(v, "f", 1) + 1)
                product(tile(v, 2, i), lambda k: hT[:, k, :])
                n = WQ_TILES * v + i
                wait_read(pe, tile(v, 2, i))
                transposes(batch(v, "wq", i), [qtok[:, j * P:(j + 1) * P] for j in range(4)])
                pe.wait_ge(t_copied, batch(v, "wq", i) + 1)
                if n:
                    pe.wait_ge(S_in, n)
                for j in range(4):
                    last = nc.tensor.matmul(pS[:, j * P:(j + 1) * P], qhT[:, j, :], keyT[:, layer, j % 2, :],
                                            start=True, stop=True)
                last.then_inc(keyed, 1)

            def gather(v, g):
                n = v * GG + g
                pe.wait_ge(diag_ready, n + 1)
                if g == 0 and v:
                    pe.wait_ge(x_summed, 2 * v)
                for s in range(GS):
                    j = n * GS + s
                    for half in range(2):
                        last = nc.tensor.matmul(acc[half][:, :], diag[:, n % 2, s, :],
                                                ring[:, j % RING, D + half * NT:D + (half + 1) * NT],
                                                start=g == 0 and s == 0, stop=g == GG - 1 and s == GS - 1)
                    last.then_inc(summed, 1)

            stages = {"mod": mod_, "norm": norm, "in": in_, "qknorm": qknorm, "pool": pool_, "head": head,
                      "attout": attout, "out": out_, "wq": wq, "gather": gather}
            for name, v, i in order:
                if name in stages:
                    stages[name](v, i)

        @block.scalar
        def _(act):
            act.wait_ge(consts, CONSTS)
            nc.scalar.activation(silu[:, 0, :], cT, ACT.Exp, scale=-1.0).then_inc(silu_step, 1)

            def mod_(layer, i):
                n = MOD_TILES * layer + i
                if n >= 2:
                    before = divmod(n - 2, MOD_TILES)
                    wait_read(act, mod_tile(*before))
                    if before[1] // 2 in GAIN_PARTS:
                        act.wait_ge(scaled, gains_until(*before))
                if layer and i == 0:
                    act.wait_ge(routed, CHUNKS)
                part, half = divmod(i, 2)
                columns = slice(i * NT, (i + 1) * NT)
                act.dma_start(brow[:, n % 2, :], a["ada_b"][layer, columns].unsqueeze(0).to_broadcast([P, NT]))\
                    .then_inc(brow_in[n % 2], 16)
                if part in GAIN_PARTS:
                    gain = a["norm_mix_g" if part == 1 else "norm_ffn_g"][layer, half * NT:(half + 1) * NT]
                    act.dma_start(grow[:, n % 2, :], gain.unsqueeze(0).to_broadcast([P, NT]))\
                        .then_inc(brow_in[n % 2], 16)

            def norm(v, which):
                if which:
                    act.wait_ge(half_done, 2 * (tile(v, 0, mix_tiles(v // CHUNKS) - 1) + 1))
                else:
                    act.wait_ge(half_done, 2 * tile(v, 0, 0))
                for i in range(2):
                    b = batch(v, "f" if which else "h", i)
                    act.wait_ge(t_done, b + 1)
                    nc.scalar.activation(hT[:, 4 * i:4 * i + 4, :], pT[b % 2][:, :].rearrange("p (k t) -> p k t", t=P),
                                         ACT.Copy).then_inc(t_copied, 1)

            def in_(v, i):
                layer, c = divmod(v, CHUNKS)
                t = tile(v, 0, i)
                if layer == 0:
                    act.wait_ge(half_done, 2 * t + 2)
                    if i == 0:
                        act.wait_ge(scaled, 4)
                        wait_read(act, mod_tile(0, MOD_TILES - 1))
                        if v:
                            act.wait_ge(routed, v)
                    dst = (qk[:, 0:NT], qk[:, NT:2 * NT], vtok[:, c, :], utok[:, c, :])[i]
                    nc.scalar.activation(dst, pG[t % 2][:, :], ACT.Copy).then_inc(g_read[t % 2], 1)
                    return
                half, what = divmod(i, 3)
                n = 2 * c + half
                if what == 0:
                    act.wait_ge(half_done, 2 * t + 2)
                    if i == 0:
                        act.wait_ge(scaled, 8)
                        wait_read(act, mod_tile(1, MOD_TILES - 1))
                        act.wait_ge(routed, v)
                    if n:
                        wait_read(act, tile(v, 0, 1) if half else tile(v - 1, 0, 4))
                    nc.scalar.activation(xin, pG[t % 2][:, :], ACT.Copy).then_inc(g_read[t % 2], 1)
                elif what == 2:
                    act.wait_ge(half_done, 2 * t + 2)
                    if n:
                        act.wait_ge(t_done, batch(v, "ub", 1) + 1 if half else batch(v - 1, "ub", 3) + 1)
                    nc.scalar.activation(bhalf, pG[t % 2][:, :], ACT.Copy).then_inc(g_read[t % 2], 1)
                    for k, dst in enumerate((uT[:, 4 * half:4 * half + 4, 2:P + 2], bT[:, 4 * half:4 * half + 4, :])):
                        b = batch(v, "ub", 2 * half + k)
                        act.wait_ge(t_done, b + 1)
                        if c and half == 0 and k == 0:
                            act.wait_ge(zT_ready, CHUNKS + 1)
                            act.wait_ge(shifted, 1)
                        nc.scalar.activation(dst, pT[b % 2][:, :].rearrange("p (k t) -> p k t", t=P),
                                             ACT.Copy).then_inc(t_copied, 1)

            def qknorm(v, _):
                c = v % CHUNKS
                for i, (gain, dst) in enumerate(((qgain, qT), (kgain, kT[:, :, c * P:(c + 1) * P]))):
                    b = batch(v, "qk", i)
                    act.wait_ge(t_done, b + 1)
                    for j in range(4):
                        last = nc.scalar.activation(dst[:, j, :], pT[b % 2][:, j * P:(j + 1) * P], ACT.Copy,
                                                    scale=gain[:, j:j + 1])
                    last.then_inc(t_copied, 1)

            def pool_(v, _):
                act.wait_ge(diff_done, v + 1)
                nc.scalar.activation(dT, pS[:, :].rearrange("p (g t) -> p g t", g=GROUPS), ACT.Copy).then_inc(dT_ready, 1)
                act.wait_ge(pooled, v + 1)
                for g in range(GROUPS):
                    last = nc.scalar.activation(zT[:, 4 + g, :], pO[:, g * P:(g + 1) * P], ACT.Copy,
                                                scale=pscale[:, g:g + 1])
                last.then_inc(zT_ready, 1)

            def head(v, i):
                c = v % CHUNKS
                keys = (c + 1) * P
                n = HEADS * v + i
                act.wait_ge(maxed, n + 1)
                if i >= 2:
                    act.wait_ge(t_done, batch(v, "p", i - 2) + 1)
                nc.scalar.activation(pr[:, i % 2, 0:keys], sc[:, i % 2, 0:keys], ACT.Exp, bias=att[:, 1, i:i + 1],
                                     accum_out=att[:, 2, i:i + 1]).then_inc(expd, 1)
                b = batch(v, "p", i)
                act.wait_ge(t_done, b + 1)
                if i >= 2:
                    act.wait_ge(pv_done, n - 1)
                nc.scalar.activation(prT[:, i % 2, 0:c + 1, :],
                                     pT[b % 2][:, 0:keys].rearrange("p (k t) -> p k t", t=P),
                                     ACT.Copy).then_inc(t_copied, 1)

            def attout(v, _):
                b = batch(v, "o")
                act.wait_ge(t_done, b + 1)
                nc.scalar.activation(zT[:, 0:4, :], pT[b % 2][:, :].rearrange("p (k t) -> p k t", t=P),
                                     ACT.Copy).then_inc(t_copied, 1)

            def wq(v, i):
                t = tile(v, 2, i)
                n = WQ_TILES * v + i
                act.wait_ge(half_done, 2 * t + 2)
                if i == 0:
                    act.wait_ge(x_mixed, OUT_TILES * v + OUT_TILES)
                nc.scalar.activation(qtok, pG[t % 2][:, :], ACT.Copy).then_inc(g_read[t % 2], 1)
                b = batch(v, "wq", i)
                act.wait_ge(t_done, b + 1)
                nc.scalar.activation(qhT, pT[b % 2][:, :].rearrange("p (k t) -> p k t", t=P),
                                     ACT.Copy).then_inc(t_copied, 1)
                act.wait_ge(keyed, n + 1)
                nc.scalar.activation(S[:, 2 * i:2 * i + 2, :, :],
                                     pS[:, :].rearrange("p (h s n) -> p h s n", h=2, s=2), ACT.Copy).then_inc(S_in, 1)

            def pick(v, _):
                act.wait_ge(masked, v + 1)
                nc.scalar.activation(gates[:, v % 2, :], gates[:, v % 2, :], ACT.Exp).then_inc(gexp, 1)

            def gather(v, g):
                n = v * GG + g
                act.wait_ge(dotted, n + 1)
                nc.scalar.activation(gel[:, n % 2, :], dots[:, n % 2, :], ACT.Gelu).then_inc(gelued, 1)

            stages = {"mod": mod_, "norm": norm, "in": in_, "qknorm": qknorm, "pool": pool_, "head": head,
                      "attout": attout, "wq": wq, "pick": pick, "gather": gather}
            for name, v, i in order:
                if name in stages:
                    stages[name](v, i)

        @block.vector
        def _(dve):
            steps = [0]

            def link(ins):
                steps[0] += 1
                ins.then_inc(chain, 1)
                dve.wait_ge(chain, steps[0])

            dve.wait_ge(silu_step, 1)
            nc.vector.tensor_scalar(silu[:, 1, :], silu[:, 0, :], 1.0, None, ALU.add).then_inc(silu_step, 1)
            dve.wait_ge(silu_step, 2)
            nc.vector.reciprocal(silu[:, 1, :], silu[:, 1, :]).then_inc(silu_step, 1)
            dve.wait_ge(silu_step, 3)
            link(nc.vector.tensor_tensor(silu[:, 2, :], cT, silu[:, 1, :], ALU.mult))

            def spread_silu():
                nc.vector.tensor_copy(cact[:, :, :], silu[:, 2, :].unsqueeze(2).to_broadcast([P, KC, P]))\
                    .then_inc(silu_step, 1)

            spread_silu()

            def rsqrt(y, v_, t):
                link(nc.vector.tensor_scalar(y.bitcast(I32), v_.bitcast(I32), -0.5, float(0x5F3759DF), ALU.mult, ALU.add))
                for _ in range(4):
                    link(nc.vector.tensor_tensor(t, y, y, ALU.mult))
                    link(nc.vector.tensor_tensor(t, t, v_, ALU.mult))
                    link(nc.vector.tensor_scalar(t, t, -0.5, 1.5, ALU.mult, ALU.add))
                    link(nc.vector.tensor_tensor(y, y, t, ALU.mult))

            def mod_(layer, i):
                if layer and i == 0:
                    dve.wait_ge(half_done, 2 * tile(CHUNKS - 1, 2, WQ_TILES - 1) + 2)
                    spread_silu()
                t = mod_tile(layer, i)
                n = MOD_TILES * layer + i
                part, half = divmod(i, 2)
                row = 6 if (layer and part == 5) else part
                dst = mod[:, row, half * NT:(half + 1) * NT]
                dve.wait_ge(brow_in[n % 2], rows_landed(n))
                dve.wait_ge(half_done, 2 * t + 2)
                ins = nc.vector.tensor_tensor(dst, pG[t % 2][:, :], brow[:, n % 2, :], ALU.add)
                ins.then_inc(g_read[t % 2], 1)
                wait_read(dve, t)
                if part in GAIN_PARTS:
                    ins = nc.vector.scalar_tensor_tensor(out=dst, in0=dst, scalar=1.0, in1=grow[:, n % 2, :],
                                                         op0=ALU.add, op1=ALU.mult)
                    ins.then_inc(scaled, 1)

            def norm(v, which):
                layer, c = divmod(v, CHUNKS)
                if v == 0 and which == 0:
                    dve.wait_ge(consts, CONSTS)
                if which == 0:
                    dve.wait_ge(scaled, 4 * (layer + 1))
                    wait_read(dve, mod_tile(layer, MOD_TILES - 1))
                else:
                    dve.wait_ge(x_mixed, OUT_TILES * (v + 1))
                src = x[:, c, :]
                dst = h2[:, c, :] if which else hm[:, :]
                link(nc.vector.tensor_tensor_reduce(out=dst, in0=src, in1=src, scale=1.0, scalar=0.0,
                                                    op0=ALU.mult, op1=ALU.add, accum_out=ss))
                link(nc.vector.tensor_scalar(ve, ss, 1.0 / D, EPS, ALU.mult, ALU.add))
                rsqrt(rs, ve, r2)
                link(nc.vector.scalar_tensor_tensor(out=dst, in0=src, scalar=rs, in1=mod[:, 4 if which else 1, :],
                                                    op0=ALU.mult, op1=ALU.mult))
                nc.vector.tensor_tensor(dst, dst, mod[:, 3 if which else 0, :], ALU.add).then_inc(h_ready, 1)
                dve.wait_ge(h_ready, 2 * v + which + 1)

            def in_(v, i):
                layer, c = divmod(v, CHUNKS)
                if layer and i % 3 == 1:
                    half = i // 3
                    n = 2 * c + half
                    t = tile(v, 0, i)
                    dve.wait_ge(half_done, 2 * t + 2)
                    wait_read(dve, tile(v, 0, 3 * half))
                    if n:
                        dve.wait_ge(t_done, batch(v, "ub", 0) + 1 if half else batch(v - 1, "ub", 2) + 1)
                    nc.vector.tensor_tensor(uhalf, pG[t % 2][:, :], xin, ALU.mult)\
                        .then_inc(g_read[t % 2], 1)

            def qknorm(v, _):
                wait_read(dve, tile(v, 0, 0))
                wait_read(dve, tile(v, 0, 1))
                h16 = qk.rearrange("p (h d) -> p h d", d=HD)
                link(nc.vector.tensor_tensor(hm[:, :], qk, qk, ALU.mult))
                link(nc.vector.tensor_reduce(ssq, hm[:, :].rearrange("p (h d) -> p h d", d=HD), axis=AX.X, op=ALU.add))
                link(nc.vector.tensor_scalar(veq, ssq, 1.0 / HD, EPS, ALU.mult, ALU.add))
                rsqrt(rsq, veq, r2q)
                link(nc.vector.tensor_scalar(rsq[:, 0:HEADS], rsq[:, 0:HEADS], HD ** -0.5, None, ALU.mult))
                nc.vector.tensor_tensor(h16, h16, rsq.unsqueeze(2).to_broadcast([P, 2 * HEADS, HD]), ALU.mult)\
                    .then_inc(qk_ready, 1)

            def head(v, i):
                c = v % CHUNKS
                keys = (c + 1) * P
                n = HEADS * v + i

                def masked_max(h):
                    m = HEADS * v + h
                    dve.wait_ge(scored, m + 1)
                    if h == 0:
                        dve.wait_ge(pooled, v + 1)
                    if h >= 2:
                        dve.wait_ge(expd, m - 1)
                    link(nc.vector.tensor_tensor_reduce(
                        out=sc[:, h % 2, 0:keys], in0=score_bank[h % 2][:, 0:keys],
                        in1=bias[:, c * P:c * P + keys], scale=1.0, scalar=LOWEST, op0=ALU.add, op1=ALU.max,
                        accum_out=att[:, 0, h:h + 1]))
                    nc.vector.tensor_scalar(att[:, 1, h:h + 1], att[:, 0, h:h + 1], -1.0, None, ALU.mult)\
                        .then_inc(maxed, 1)

                if i == 0:
                    masked_max(0)
                if i + 1 < HEADS:
                    masked_max(i + 1)

            def attout(v, _):
                dve.wait_ge(expd, HEADS * (v + 1))
                link(nc.vector.reciprocal(att[:, 3, :], att[:, 2, :]))
                dve.wait_ge(pv_done, HEADS * (v + 1))
                nc.vector.tensor_tensor(otok.rearrange("p (h d) -> p h d", d=HD),
                                        pO[:, :].rearrange("p (h d) -> p h d", d=HD),
                                        att[:, 3, :].unsqueeze(2).to_broadcast([P, HEADS, HD]), ALU.mult)\
                    .then_inc(otok_ready, 1)

            def conv(v, _):
                c = v % CHUNKS
                dve.wait_ge(t_copied, batch(v, "ub", 3) + 1)
                if c == 0:
                    link(nc.vector.memset(uT[:, :, 0:2], 0.0))

                def w(lag):
                    return convw[:, lag, :].unsqueeze(2).to_broadcast([P, KC, P])

                link(nc.vector.tensor_tensor(zT, uT[:, :, 2:P + 2], w(0), ALU.mult))
                for lag in (1, 2):
                    link(nc.vector.tensor_tensor(lagT, uT[:, :, 2 - lag:P + 2 - lag], w(lag), ALU.mult))
                    link(nc.vector.tensor_tensor(zT, zT, lagT, ALU.add))
                if c == 0:
                    nc.vector.tensor_copy(uT[:, :, 0:2], uT[:, :, P:P + 2]).then_inc(shifted, 1)
                nc.vector.tensor_tensor(zT, zT, bT, ALU.mult).then_inc(zT_ready, 1)

            def out_(v, i):
                c = v % CHUNKS
                t = tile(v, 1, i)
                dve.wait_ge(half_done, 2 * t + 2)
                cols_ = slice(i * NT, (i + 1) * NT)
                if i:
                    dve.wait_ge(x_mixed, OUT_TILES * v + i)
                ins = nc.vector.tensor_tensor(ytmp, pG[t % 2][:, :], mod[:, 2, cols_], ALU.mult)
                ins.then_inc(g_read[t % 2], 1)
                wait_read(dve, t)
                nc.vector.tensor_tensor(x[:, c, cols_], x[:, c, cols_], ytmp, ALU.add).then_inc(x_mixed, 1)

            def top16(values, spare, best, where):
                link(nc.vector.max(best[:, 0:8], values))
                link(nc.vector.max_index(where[:, 0:8], best[:, 0:8], values))
                link(nc.vector.match_replace(spare, best[:, 0:8], values, LOWEST))
                link(nc.vector.max(best[:, 8:16], spare))
                link(nc.vector.max_index(where[:, 8:16], best[:, 8:16], spare))

            def route(v, h):
                dve.wait_ge(S_in, WQ_TILES * v + h // 2 + 1)
                for s in range(2):
                    top16(S[:, h, s, :], s2, v16[:, h, s, :], i16[:, h, s, :])
                link(nc.vector.tensor_tensor(cand.rearrange("p (a b) -> p a b", a=PK),
                                             v16[:, h, 0, :].unsqueeze(2).to_broadcast([P, PK, PK]),
                                             v16[:, h, 1, :].unsqueeze(1).to_broadcast([P, PK, PK]), ALU.add))
                top16(cand, cand2, vs[:, h, :], ci[:, h, :])

            def pick(v, _):
                gat = gates[:, v % 2, :].rearrange("p (h k) -> p h k", h=PH)
                nc.vector.tensor_tensor(gat, vs[:, :, :], vs[:, :, 0:1].to_broadcast([P, PH, PK]), ALU.subtract)\
                    .then_inc(masked, 1)
                flat = ci[:, :, :].rearrange("p h k -> p (h k)")
                link(nc.vector.tensor_single_scalar(cab[:, 0, :], flat, 4, op=ALU.logical_shift_right))
                link(nc.vector.tensor_single_scalar(cab[:, 1, :], flat, PK - 1, op=ALU.bitwise_and))
                half = SLOTS // 2
                for part in range(2):
                    for s in range(2):
                        places = cab[:, s, part * half:(part + 1) * half]
                        hotv = hot.rearrange("p (j a) -> p j a", a=PK)
                        link(nc.vector.tensor_tensor(hotv, places.unsqueeze(2).to_broadcast([P, half, PK]),
                                                     iota[:, :].unsqueeze(1).to_broadcast([P, half, PK]), ALU.is_equal))
                        hot4 = hot.rearrange("p (h j a) -> p h j a", h=PH // 2, a=PK)
                        kept = i16[:, part * PH // 2:(part + 1) * PH // 2, s, :]
                        link(nc.vector.tensor_tensor(hot4, hot4, kept.unsqueeze(2).to_broadcast([P, PH // 2, PK, PK]),
                                                     ALU.mult))
                        link(nc.vector.tensor_reduce(sub[:, s, part * half:(part + 1) * half],
                                                     hotv, axis=AX.X, op=ALU.add))
                dve.wait_ge(gexp, v + 1)
                link(nc.vector.tensor_reduce(gsum[:, 0, :], gat, axis=AX.X, op=ALU.add))
                link(nc.vector.reciprocal(gsum[:, 1, :], gsum[:, 0, :]))
                link(nc.vector.tensor_tensor(gat, gat, gsum[:, 1, :].unsqueeze(2).to_broadcast([P, PH, PK]), ALU.mult))
                nc.vector.scalar_tensor_tensor(out=ids[:, v % 2, :], in0=sub[:, 0, :], scalar=float(NKEY),
                                               in1=sub[:, 1, :], op0=ALU.mult, op1=ALU.add)\
                    .then_inc(routed, 1)
                dve.wait_ge(routed, v + 1)

            def gather(v, g):
                n = v * GG + g
                for s in range(GS):
                    j = n * GS + s
                    dve.wait_ge(row_in[j % RING], 16 * (j // RING + 1))
                    last = nc.vector.tensor_tensor_reduce(
                        out=ring[:, j % RING, 0:D], in0=ring[:, j % RING, 0:D], in1=h2[:, v % CHUNKS, :], scale=1.0,
                        scalar=0.0, op0=ALU.mult, op1=ALU.add, accum_out=dots[:, n % 2, s:s + 1])
                last.then_inc(dotted, 1)
                dve.wait_ge(gelued, n + 1)
                link(nc.vector.tensor_tensor(coef[:, n % 2, :], gel[:, n % 2, :],
                                             gates[:, v % 2, g * GS:(g + 1) * GS], ALU.mult))
                if n >= 2:
                    dve.wait_ge(summed, GS * (n - 1))
                for s in range(GS):
                    last = nc.vector.tensor_scalar(diag[:, n % 2, s, :], ident[:, :], coef[:, n % 2, s:s + 1],
                                                   None, ALU.mult)
                last.then_inc(diag_ready, 1)

            def finish(v, _):
                layer, c = divmod(v, CHUNKS)
                dve.wait_ge(summed, SLOTS * (v + 1))
                for half in range(2):
                    cols_ = slice(half * NT, (half + 1) * NT)
                    ins = nc.vector.tensor_tensor(otmp, acc[half][:, :], mod[:, 6 if layer else 5, cols_], ALU.mult)
                    link(ins)
                    ins = nc.vector.tensor_tensor(x[:, c, cols_], x[:, c, cols_], otmp, ALU.add)
                    ins.then_inc(x_summed, 1)
                    dve.wait_ge(x_summed, 2 * v + half + 1)

            stages = {"mod": mod_, "norm": norm, "in": in_, "qknorm": qknorm, "head": head, "attout": attout,
                      "conv": conv, "out": out_, "route": route, "pick": pick, "gather": gather, "finish": finish}
            for name, v, i in order:
                if name in stages:
                    stages[name](v, i)


def shape_constants():
    import numpy as np

    seq = P * CHUNKS
    t = np.arange(seq)
    gap = t[:, None] - t[None, :]
    reach = np.zeros((seq, seq))
    for window, dil in ((128, 1), (512, 4), (2048, 16)):
        reach += (gap >= 0) & (gap % dil == 0) & (gap <= window)
    bias = np.where(reach > 0, np.log(np.maximum(reach, 1)), MASKED).astype(np.float32)
    bias = np.concatenate([bias[:P, :P], bias[P:, :]], axis=1)
    mean = np.zeros((GROUPS, seq, seq))
    for g, w in enumerate(WINDOWS):
        mean[g] = ((gap >= 0) & (gap < w)).T / np.minimum(t + 1, w)[None, :] - np.eye(seq)
    poolm = np.stack([mean[:, :P, :P], mean[:, P:, P:], mean[:, :P, P:]])
    return {
        "ident": np.eye(P, dtype=np.float32),
        "bias": np.ascontiguousarray(bias),
        "poolm": np.ascontiguousarray(poolm.transpose(2, 0, 1, 3).astype(np.float32)),
        "iota": np.tile(np.arange(PK, dtype=np.float32), (P, 1)),
    }


def kernel(**inputs):
    import numpy as np
    import concourse.bacc as bacc
    from concourse.bass_utils import run_bass_kernel_spmd

    def columns(a):
        return np.asarray(a).reshape(-1, P).T

    given = {k: np.asarray(v) for k, v in inputs.items()}
    arrays = {k: given[k] for k in ("x", "ada_w", "ada_b", "norm_mix_g", "norm_ffn_g", "ab_w_in", "pool_w",
                                    "ab_w_out", "conv_w_in", "conv_w_out", "peer_w_q")}
    for layer in range(LAYERS):
        arrays[f"uv{layer}"] = np.concatenate([given["peer_u"][layer], given["peer_v"][layer]], axis=1)
    arrays["keyT"] = np.stack([given["peer_key1"], given["peer_key2"]], axis=1).transpose(3, 0, 1, 2)
    arrays["cols"] = np.concatenate([columns(given["c"]), columns(given["ab_q_gain"]), columns(given["ab_k_gain"]),
                                     columns(given["pool_scale"]), columns(given["conv_w"])], axis=1)
    arrays.update(shape_constants())

    nc = bacc.Bacc("TRN2", target_bir_lowering=False, num_devices=1)
    maps, aps = {}, {}
    for name, a in arrays.items():
        maps[f"in_{name}"] = np.ascontiguousarray(a)
        aps[name] = nc.dram_tensor(f"in_{name}", a.shape, mybir.dt.from_np(a.dtype), kind="ExternalInput").ap()
    out = nc.dram_tensor("out_x", given["x"].shape, F32, kind="ExternalOutput").ap()
    trunk(nc, aps, out)
    r = run_bass_kernel_spmd(nc, [maps], core_ids=[0])
    return r.results[0]["out_x"]
```

```python
from contextlib import ExitStack

import concourse.bass as bass
from concourse import mybir
from concourse.alu_op_type import AluOpType as ALU

F32 = mybir.dt.float32
I32 = mybir.dt.int32
U32 = mybir.dt.uint32
ACT = mybir.ActivationFunctionType
AX = mybir.AxisListType

P = 128
D = 1024
KC = D // P
NT = 512
LAYERS = 2
CHUNKS = 2
HEADS, HD = 8, 64
WINDOWS = (2, 4, 8, 16)
GROUPS = len(WINDOWS)
CONV = 3
PH, PK = 8, 16
NKEY = 128
EPS = 1e-6
LOWEST = -3.0e38
MASKED = -1.0e30
SLOTS = PH * PK
SPARE_GROUPS = 6
COST = {"modpart": 2.0, "mod": 1.7, "norm": 5.0, "in": 3.4, "inread": 1.0, "out": 3.4, "outread": 1.3, "wq": 3.4,
        "wqread": 2.0, "qknorm": 7.0, "pool": 4.0, "head": 3.0, "attout": 1.5, "conv": 8.0, "route": 1.5,
        "pick": 4.0, "gate": 1.0}
RING = 8
GS = 2
GG = SLOTS // GS
WR = 5

MOD_TILES = 6 * D // NT
MIX0_TILES = 4
MIX1_TILES = 6
OUT_TILES = D // NT
WQ_TILES = 2 * PH * P // NT
HPT = PH // WQ_TILES
CONV_ORDER = (0, 4, 2, 1, 5, 3)
GAIN_PARTS = (1, 4)


def mix_tiles(layer):
    return MIX1_TILES if layer else MIX0_TILES


TB0 = {"h": 0, "qk": 2, "p": 4, "o": 4 + HEADS, "f": 5 + HEADS, "wq": 7 + HEADS, "end": 7 + HEADS + WQ_TILES}
TB1 = {"h": 0, "ub": 2, "f": 6, "wq": 8, "end": 8 + WQ_TILES}


def batch(v, name, i=0):
    layer, c = divmod(v, CHUNKS)
    of = TB1 if layer else TB0
    return (CHUNKS * TB0["end"] if layer else 0) + c * of["end"] + of[name] + i


def trunk(nc, a, out):
    def mods(layer, parts):
        return [(n, layer, 2 * part + half) for part in parts for half in range(2) for n in ("modpart", "mod")]

    def products(name, v, i):
        return [(name, v, 2 * i), (name, v, 2 * i + 1), (name + "read", v, i)]

    def before_attention(v):
        return [("norm", v, 0)] + [s for i in range(MIX0_TILES) for s in products("in", v, i)]

    def attention(v):
        return [("qknorm", v, 0), ("pool", v, 0)] + [("head", v, i) for i in range(HEADS)] + [("attout", v, 0)]

    def convolution(v):
        return [("norm", v, 0)] + [s for i in range(MIX1_TILES) for s in products("in", v, i)] + [("conv", v, 0)]

    def projection(v):
        return [s for i in range(OUT_TILES) for s in products("out", v, i)]

    def experts(v):
        steps = [("norm", v, 1)]
        for i in range(WQ_TILES):
            steps += products("wq", v, i)
            steps += [("route", v, 3 * h + k) for h in range(HPT * i, HPT * i + HPT) for k in range(3)]
            steps += [("pick", v, i), ("gate", v, i)]
        return steps

    def woven(v, other):
        steps, total, spent, at = [], sum(COST[s[0]] for s in other), 0.0, 0
        for g in range(GG):
            steps.append(("gather", v, g))
            if g == 0 and v:
                steps.append(("finish", v - 1, 0))
            while at < len(other) and spent <= total * (g + 1) / (GG - SPARE_GROUPS):
                spent += COST[other[at][0]]
                steps.append(other[at])
                at += 1
        return steps

    order = mods(0, (0, 1)) + before_attention(0) + mods(0, (2,)) + attention(0) + projection(0)
    order += mods(0, (3, 4, 5)) + experts(0)
    order += woven(0, before_attention(1) + attention(1) + projection(1) + experts(1))
    order += woven(1, mods(1, range(6)) + convolution(2) + projection(2) + experts(2))
    order += woven(2, convolution(3) + projection(3) + experts(3))
    order += woven(3, []) + [("finish", 3, 0)]

    number, load, source, banked = {}, {}, [], [[] for _ in range(4)]
    for name, v, i in order:
        if name in ("modpart", "mod"):
            key = (name, v, i)
        elif name in ("in", "out", "wq") and i % 2 == 0:
            key = (name, v, i // 2)
        else:
            if name == "head" and i == 0:
                banked[v] = [len(number) - 2, len(number) - 1]
            continue
        number[key] = len(number)
        if name == "mod":
            continue
        load[key] = len(source)
        layer = v if name == "modpart" else v // CHUNKS
        source.append({
            "modpart": lambda: (a["ada_w"][layer], i),
            "in": lambda: (a["conv_w_in"][0], CONV_ORDER[i // 2]) if layer else (a["ab_w_in"][0], i // 2),
            "out": lambda: ((a["conv_w_out"] if layer else a["ab_w_out"])[0], i // 2),
            "wq": lambda: (a["peer_w_q"][layer], i // 2),
        }[name]())

    ctx = ExitStack()
    with ctx:
        def sb(name, shape, dt=F32):
            return ctx.enter_context(nc.sbuf_tensor("t_" + name, shape, dt))

        def pb(name, shape):
            return ctx.enter_context(nc.psum_tensor("p_" + name, shape, F32))

        def sem(name):
            return ctx.enter_context(nc.semaphore("s_" + name))

        ring = sb("ring", [P, RING, 2 * D])
        wring = sb("wring", [P, WR, KC // 2, NT])
        x = sb("x", [P, CHUNKS, D])
        mod = sb("mod", [P, 7, D])
        h2 = sb("h2", [P, CHUNKS, D])
        hT = sb("hT", [P, KC, P])
        hm = sb("hm", [P, D])
        zT = hm[:, :].rearrange("p (k t) -> p k t", k=KC)
        ident = sb("ident", [P, P])
        bias = sb("bias", [P, 3 * P])
        poolm = sb("poolm", [P, 3, GROUPS, P])
        poolw = sb("poolw", [P, GROUPS, P])
        keyT = sb("keyT", [P, LAYERS, 2, P])
        cols = sb("cols", [P, KC + 3 * 4 + CONV * KC])
        cT = cols[:, 0:8]
        qgain, kgain, pscale = cols[:, 8:12], cols[:, 12:16], cols[:, 16:20]
        convw = cols[:, 20:44].rearrange("p (l k) -> p l k", l=CONV)
        iota = sb("iota", [P, PK])
        silu = sb("silu", [P, 3, KC])
        quads = sb("quads", [P, 1])
        adab = sb("adab", [LAYERS * MOD_TILES, NT])
        modsum = sb("modsum", [P, NT])

        keep = sb("keep", [P, 3104])
        kT = keep[:, 0:1024].rearrange("p (j t) -> p j t", j=4)
        vtok = keep[:, 1024:2048].rearrange("p (c n) -> p c n", c=CHUNKS)
        utok = keep[:, 2048:3072].rearrange("p (c n) -> p c n", c=CHUNKS)
        uT = keep[:, 0:1040].rearrange("p (k t) -> p k t", k=KC)
        bT = keep[:, 1040:2064].rearrange("p (k t) -> p k t", k=KC)
        lagT = keep[:, 2064:3088].rearrange("p (k t) -> p k t", k=KC)
        work = sb("work", [P, 3072])
        qk = work[:, 0:1024]
        otok = work[:, 0:512]
        qT = work[:, 1024:1536].rearrange("p (j t) -> p j t", j=4)
        sc = work[:, 1536:2048].rearrange("p (b t) -> p b t", b=2)
        dT = work[:, 1536:2048].rearrange("p (g t) -> p g t", g=GROUPS)
        pr = work[:, 2048:2560].rearrange("p (b t) -> p b t", b=2)
        prT = work[:, 2560:3072].rearrange("p (b k t) -> p b k t", b=2, k=2)
        xin, uhalf, bhalf = work[:, 0:512], work[:, 512:1024], work[:, 1024:1536]
        ytmp = work[:, 2048:2560]
        S = work[:, 0:2048].rearrange("p (h s n) -> p h s n", h=PH, s=2)
        qtok = work[:, 2048:2560]
        qhT = work[:, 2560:3072].rearrange("p (j t) -> p j t", j=4)
        cand, cand2 = hm[:, 0:256], hm[:, 256:512]
        s2 = hm[:, 256:384]
        hot = hm[:, 512:1024]

        v16 = sb("v16", [P, PH, 2, PK])
        i16 = sb("i16", [P, PH, 2, PK], U32)
        vs = sb("vs", [P, PH, PK])
        ci = sb("ci", [P, PH, PK], U32)
        cab = sb("cab", [P, 2, HPT * PK], U32)
        sub = sb("sub", [P, 2, HPT * PK])
        ids = sb("ids", [P, 2, SLOTS], U32)
        gates = sb("gates", [P, 2, SLOTS])
        small = sb("small", [P, 96])
        ss, ve, rs, r2 = small[:, 0:1], small[:, 1:2], small[:, 2:3], small[:, 3:4]
        ssq, veq, rsq, r2q = small[:, 16:32], small[:, 32:48], small[:, 48:64], small[:, 64:80]
        att = sb("att", [P, 4, HEADS])
        gsum = sb("gsum", [P, 2, PH])
        dots = sb("dots", [P, 2, GS])
        gel = sb("gel", [P, 2, GS])
        coef = sb("coef", [P, 2, GS])
        diag = sb("diag", [P, 2, GS, P])
        otmp = diag[:, :, :, :].rearrange("p b s t -> p (b s t)")

        acc = [pb(f"acc{i}", [P, NT]) for i in range(2)]
        pG = [pb(f"g{i}", [P, NT]) for i in range(2)]
        pT = [pb(f"t{i}", [P, NT]) for i in range(2)]
        pS = pb("s", [P, NT])
        pO = pb("o", [P, NT])
        score_bank = (pS, pG[1])

        consts = sem("consts")
        w_in = [sem(f"w_in{i}") for i in range(WR)]
        loads_used = sem("loads_used")

        t_done = sem("t_done")
        g_read = [sem(f"g_read{i}") for i in range(2)]
        t_copied = sem("t_copied")
        gain_in = sem("gain_in")
        mod_done = sem("mod_done")
        silu_step = sem("silu_step")
        chain = sem("chain")
        h_ready = sem("h_ready")
        qk_ready = sem("qk_ready")
        scored = sem("scored")
        maxed = sem("maxed")
        masked = sem("masked")
        expd = sem("expd")
        pv_done = sem("pv_done")
        otok_ready = sem("otok_ready")
        diff_done = sem("diff_done")
        dT_ready = sem("dT_ready")
        pooled = sem("pooled")
        zT_ready = sem("zT_ready")
        x_mixed = sem("x_mixed")
        keyed = sem("keyed")
        S_in = sem("S_in")
        shifted = sem("shifted")
        gexp = sem("gexp")
        routed = sem("routed")
        row_in = [sem(f"row_in{i}") for i in range(RING)]
        dotted = sem("dotted")
        gelued = sem("gelued")
        diag_ready = sem("diag_ready")
        summed = sem("summed")
        x_summed = sem("x_summed")
        stored = sem("stored")

        CONSTS = 16 * 10

        def wait_product(engine, *key):
            engine.wait_ge(loads_used, 2 * load[key] + 2)

        def wait_read(engine, t):
            engine.wait_ge(g_read[t % 2], t // 2 + 1)

        block = ctx.enter_context(nc.Block())

        @block.sync
        def _(sp):
            sp.dma_start(cols[:, :], a["cols"]).then_inc(consts, 16)

            def load_weights(t):
                w, i = source[t]
                for half in range(2):
                    n = 2 * t + half
                    if n >= WR:
                        sp.wait_ge(loads_used, n - WR + 1)
                    rows = w[half * D // 2:(half + 1) * D // 2, i * NT:(i + 1) * NT]
                    sp.dma_start(wring[:, n % WR, :, :], rows.rearrange("(k p) n -> p k n", p=P))\
                        .then_inc(w_in[n % WR], 16)

            early = 2
            for t in range(early):
                load_weights(t)
            sp.dma_start(ident[:, :], a["ident"]).then_inc(consts, 16)
            sp.dma_start(quads[:, :], a["quads"]).then_inc(consts, 16)
            sp.dma_start(adab[:, :], a["ada_b"].rearrange("l (i n) -> (l i) n", n=NT)).then_inc(consts, 16)
            sp.dma_start(x[:, :, :], a["x"][0].rearrange("(c p) d -> p c d", p=P)).then_inc(consts, 16)
            for part in GAIN_PARTS:
                gain = a["norm_mix_g" if part == 1 else "norm_ffn_g"][0, :]
                sp.dma_start(mod[:, part, :], gain.unsqueeze(0).to_broadcast([P, D])).then_inc(gain_in, 16)
            sp.dma_start(bias[:, :], a["bias"]).then_inc(consts, 16)
            sp.dma_start(poolm[:, :, :, :], a["poolm"]).then_inc(consts, 16)
            sp.dma_start(poolw[:, :, :], a["pool_w"][0].rearrange("g c d -> c g d")).then_inc(consts, 16)
            sp.dma_start(keyT[:, :, :, :], a["keyT"]).then_inc(consts, 16)
            sp.dma_start(iota[:, :], a["iota"]).then_inc(consts, 16)
            for t in range(early, len(source)):
                load_weights(t)
            for c in range(CHUNKS):
                sp.wait_ge(x_summed, 2 * (CHUNKS + c + 1))
                sp.dma_start(out[0, c * P:(c + 1) * P, :], x[:, c, :]).then_inc(stored, 16)
            sp.wait_ge(stored, 16 * CHUNKS)

        @block.gpsimd
        def _(pool):
            for v in range(LAYERS * CHUNKS):
                layer = v // CHUNKS
                for j in range(SLOTS):
                    if j % (HPT * PK) == 0:
                        pool.wait_ge(routed, WQ_TILES * v + j // (HPT * PK) + 1)
                    n = v * SLOTS + j
                    if n >= RING:
                        pool.wait_ge(summed, n - RING + 1)
                    nc.gpsimd.indirect_dma_start(
                        out=ring[:, n % RING, :], out_offset=None, in_=a[f"uv{layer}"],
                        in_offset=bass.IndirectOffsetOnAxis(ap=ids[:, v % 2, j:j + 1], axis=0),
                    ).then_inc(row_in[n % RING], 16)

        @block.tensor
        def _(pe):
            pe.wait_ge(consts, CONSTS)

            def free_bank(t):
                if t >= 2:
                    wait_read(pe, t - 2)
                return pG[t % 2]

            def product(key, half, lhsT):
                t, n = number[key], 2 * load[key] + half
                bank = free_bank(t) if half == 0 else pG[t % 2]
                pe.wait_ge(w_in[n % WR], 16 * (n // WR + 1))
                for k in range(KC // 2):
                    kk = half * KC // 2 + k
                    last = nc.tensor.matmul(bank[:, :], lhsT[:, kk, :], wring[:, n % WR, k, :],
                                            start=kk == 0, stop=kk == KC - 1)
                last.then_inc(loads_used, 1)

            def transposes(b, blocks):
                if b >= 2:
                    pe.wait_ge(t_copied, b - 1)
                for i, block_ in enumerate(blocks):
                    last = nc.tensor.transpose(pT[b % 2][:, i * P:(i + 1) * P], block_, ident[:, :])
                last.then_inc(t_done, 1)

            def modpart(layer, i):
                if i == 0 and layer == 0:
                    pe.wait_ge(silu_step, 4)
                key = ("modpart", layer, i)
                t = number[key]
                bank = free_bank(t)
                for half in range(2):
                    n = 2 * load[key] + half
                    pe.wait_ge(w_in[n % WR], 16 * (n // WR + 1))
                    for q in range(4):
                        k = 4 * half + q
                        last = nc.tensor.matmul(bank[32 * q:32 * q + 32, :], silu[:, 2, k:k + 1].to_broadcast([P, 32]),
                                                wring[:, n % WR, q, :], start=half == 0, stop=half == 1,
                                                tile_position=(0, 32 * q))
                    last.then_inc(loads_used, 1)

            def mod_(layer, i):
                t = number["mod", layer, i]
                bank = free_bank(t)
                wait_read(pe, number["modpart", layer, i])
                nc.tensor.matmul(bank[:, :], quads[:, 0:1].to_broadcast([P, P]), modsum[:, :], start=True, stop=False)
                rows, row = LAYERS * MOD_TILES, MOD_TILES * layer + i
                nc.tensor.matmul(bank[:, :], ident[0:rows, row:row + 1].to_broadcast([rows, P]), adab[:, :],
                                 start=False, stop=True).then_inc(mod_done, 1)

            def norm(v, which):
                c = v % CHUNKS
                pe.wait_ge(h_ready, 2 * v + which + 1)
                src = h2[:, c, :] if which else hm[:, :]
                for i in range(2):
                    transposes(batch(v, "f" if which else "h", i),
                               [src[:, (4 * i + j) * P:(4 * i + j + 1) * P] for j in range(4)])

            def in_(v, i):
                if i == 0:
                    pe.wait_ge(t_copied, batch(v, "h", 1) + 1)
                product(("in", v, i // 2), i % 2, hT)

            def inread(v, i):
                layer, c = divmod(v, CHUNKS)
                if layer and i % 3 == 2:
                    half = i // 3
                    wait_read(pe, number["in", v, i - 1])
                    transposes(batch(v, "ub", 2 * half), [uhalf[:, j * P:(j + 1) * P] for j in range(4)])
                    wait_read(pe, number["in", v, i])
                    transposes(batch(v, "ub", 2 * half + 1), [bhalf[:, j * P:(j + 1) * P] for j in range(4)])

            def qknorm(v, _):
                pe.wait_ge(qk_ready, v + 1)
                for i in range(2):
                    transposes(batch(v, "qk", i), [qk[:, (4 * i + j) * P:(4 * i + j + 1) * P] for j in range(4)])

            def pool_(v, _):
                c = v % CHUNKS
                wait_read(pe, number["in", v, 3])
                if v:
                    pe.wait_ge(S_in, WQ_TILES * v)
                for g in range(GROUPS):
                    for s in range(c + 1):
                        which = (0 if c == 0 else 2 if s == 0 else 1)
                        last = nc.tensor.matmul(pS[:, g * P:(g + 1) * P], utok[:, s, g * P:(g + 1) * P],
                                                poolm[:, which, g, :], start=s == 0, stop=s == c)
                last.then_inc(diff_done, 1)
                pe.wait_ge(dT_ready, v + 1)
                for g in range(GROUPS):
                    last = nc.tensor.matmul(pO[:, g * P:(g + 1) * P], poolw[:, g, :], dT[:, g, :],
                                            start=True, stop=True)
                last.then_inc(pooled, 1)

            def head(v, i):
                c = v % CHUNKS
                keys = (c + 1) * P

                def scores(h):
                    n = HEADS * v + h
                    if h == 0:
                        pe.wait_ge(t_copied, batch(v, "qk", 1) + 1)
                        for t in banked[v]:
                            wait_read(pe, t)
                        pe.wait_ge(dT_ready, v + 1)
                    elif h >= 2:
                        pe.wait_ge(maxed, n - 1)
                    if h:
                        pe.wait_ge(scored, n)
                    rows = slice(HD * (h % 2), HD * (h % 2) + HD)
                    nc.tensor.matmul(score_bank[h % 2][:, 0:keys], qT[rows, h // 2, :],
                                     kT[rows, h // 2, 0:keys], start=True, stop=True).then_inc(scored, 1)

                if i == 0:
                    scores(0)
                if i + 1 < HEADS:
                    scores(i + 1)
                n = HEADS * v + i
                pe.wait_ge(expd, n + 1)
                transposes(batch(v, "p", i), [pr[:, i % 2, k * P:(k + 1) * P] for k in range(c + 1)])
                pe.wait_ge(t_copied, batch(v, "p", i) + 1)
                if i == 0:
                    pe.wait_ge(zT_ready, v + 1)
                for k in range(c + 1):
                    last = nc.tensor.matmul(pO[:, i * HD:(i + 1) * HD], prT[:, i % 2, k, :],
                                            vtok[:, k, i * HD:(i + 1) * HD], start=k == 0, stop=k == c)
                last.then_inc(pv_done, 1)

            def attout(v, _):
                pe.wait_ge(otok_ready, v + 1)
                transposes(batch(v, "o"), [otok[:, j * P:(j + 1) * P] for j in range(4)])

            def out_(v, i):
                if i == 0:
                    pe.wait_ge(zT_ready, v + 1)
                    if v < CHUNKS:
                        pe.wait_ge(t_copied, batch(v, "o") + 1)
                product(("out", v, i // 2), i % 2, zT)

            def wq(v, i):
                if i == 0:
                    pe.wait_ge(t_copied, batch(v, "f", 1) + 1)
                product(("wq", v, i // 2), i % 2, hT)

            def wqread(v, i):
                layer = v // CHUNKS
                n = WQ_TILES * v + i
                wait_read(pe, number["wq", v, i])
                transposes(batch(v, "wq", i), [qtok[:, j * P:(j + 1) * P] for j in range(4)])
                pe.wait_ge(t_copied, batch(v, "wq", i) + 1)
                if n:
                    pe.wait_ge(S_in, n)
                for j in range(4):
                    last = nc.tensor.matmul(pS[:, j * P:(j + 1) * P], qhT[:, j, :], keyT[:, layer, j % 2, :],
                                            start=True, stop=True)
                last.then_inc(keyed, 1)

            def add_values(n):
                v, g = divmod(n, GG)
                pe.wait_ge(diag_ready, n + 1)
                if g == 0 and v:
                    pe.wait_ge(x_summed, 2 * v)
                for s in range(GS):
                    j = n * GS + s
                    for half in range(2):
                        last = nc.tensor.matmul(acc[half][:, :], diag[:, n % 2, s, :],
                                                ring[:, j % RING, D + half * NT:D + (half + 1) * NT],
                                                start=g == 0 and s == 0, stop=g == GG - 1 and s == GS - 1)
                    last.then_inc(summed, 1)

            def gather(v, g):
                if g:
                    add_values(v * GG + g - 1)

            def finish(v, _):
                add_values(v * GG + GG - 1)

            stages = {"modpart": modpart, "mod": mod_, "norm": norm, "in": in_, "inread": inread, "qknorm": qknorm,
                      "pool": pool_, "head": head, "attout": attout, "out": out_, "wq": wq, "wqread": wqread,
                      "gather": gather, "finish": finish}
            for name, v, i in order:
                if name in stages:
                    stages[name](v, i)

        @block.scalar
        def _(act):
            act.wait_ge(consts, CONSTS)
            nc.scalar.activation(silu[:, 0, :], cT, ACT.Exp, scale=-1.0).then_inc(silu_step, 1)

            def modpart(layer, i):
                if layer and i == 0:
                    act.wait_ge(h_ready, 2 * CHUNKS)
                    for part in GAIN_PARTS:
                        gain = a["norm_mix_g" if part == 1 else "norm_ffn_g"][layer, :]
                        act.dma_start(mod[:, part, :], gain.unsqueeze(0).to_broadcast([P, D])).then_inc(gain_in, 16)
                t = number["modpart", layer, i]
                wait_product(act, "modpart", layer, i)
                n = MOD_TILES * layer + i
                if n:
                    act.wait_ge(mod_done, n)
                nc.scalar.activation(modsum[:, :], pG[t % 2][:, :], ACT.Copy).then_inc(g_read[t % 2], 1)

            def mod_(layer, i):
                part, half = divmod(i, 2)
                if part in GAIN_PARTS:
                    return
                t = number["mod", layer, i]
                row = 6 if layer and part == 5 else part
                act.wait_ge(mod_done, MOD_TILES * layer + i + 1)
                nc.scalar.activation(mod[:, row, half * NT:(half + 1) * NT], pG[t % 2][:, :], ACT.Copy)\
                    .then_inc(g_read[t % 2], 1)

            def norm(v, which):
                before = ("in", v, mix_tiles(v // CHUNKS) - 1) if which else ("wq", v - 1, WQ_TILES - 1)
                if which or v:
                    wait_product(act, *before)
                for i in range(2):
                    b = batch(v, "f" if which else "h", i)
                    act.wait_ge(t_done, b + 1)
                    nc.scalar.activation(hT[:, 4 * i:4 * i + 4, :], pT[b % 2][:, :].rearrange("p (k t) -> p k t", t=P),
                                         ACT.Copy).then_inc(t_copied, 1)

            def inread(v, i):
                layer, c = divmod(v, CHUNKS)
                t = number["in", v, i]
                if i == 0 and v:
                    act.wait_ge(routed, WQ_TILES * v)
                if layer == 0:
                    wait_product(act, "in", v, i)
                    dst = (qk[:, 0:NT], qk[:, NT:2 * NT], vtok[:, c, :], utok[:, c, :])[i]
                    nc.scalar.activation(dst, pG[t % 2][:, :], ACT.Copy).then_inc(g_read[t % 2], 1)
                    return
                half, what = divmod(i, 3)
                n = 2 * c + half
                if what == 0:
                    wait_product(act, "in", v, i)
                    if n:
                        wait_read(act, number["in", v, 1] if half else number["in", v - 1, 4])
                    nc.scalar.activation(xin, pG[t % 2][:, :], ACT.Copy).then_inc(g_read[t % 2], 1)
                elif what == 2:
                    wait_product(act, "in", v, i)
                    if n:
                        act.wait_ge(t_done, batch(v, "ub", 1) + 1 if half else batch(v - 1, "ub", 3) + 1)
                    nc.scalar.activation(bhalf, pG[t % 2][:, :], ACT.Copy).then_inc(g_read[t % 2], 1)
                    for k, dst in enumerate((uT[:, 4 * half:4 * half + 4, 2:P + 2], bT[:, 4 * half:4 * half + 4, :])):
                        b = batch(v, "ub", 2 * half + k)
                        act.wait_ge(t_done, b + 1)
                        if c and half == 0 and k == 0:
                            act.wait_ge(zT_ready, CHUNKS + 1)
                            act.wait_ge(shifted, 1)
                        nc.scalar.activation(dst, pT[b % 2][:, :].rearrange("p (k t) -> p k t", t=P),
                                             ACT.Copy).then_inc(t_copied, 1)

            def qknorm(v, _):
                c = v % CHUNKS
                for i, (gain, dst) in enumerate(((qgain, qT), (kgain, kT[:, :, c * P:(c + 1) * P]))):
                    b = batch(v, "qk", i)
                    act.wait_ge(t_done, b + 1)
                    for j in range(4):
                        last = nc.scalar.activation(dst[:, j, :], pT[b % 2][:, j * P:(j + 1) * P], ACT.Copy,
                                                    scale=gain[:, j:j + 1])
                    last.then_inc(t_copied, 1)

            def pool_(v, _):
                act.wait_ge(diff_done, v + 1)
                nc.scalar.activation(dT, pS[:, :].rearrange("p (g t) -> p g t", g=GROUPS), ACT.Copy).then_inc(dT_ready, 1)
                act.wait_ge(pooled, v + 1)
                for g in range(GROUPS):
                    last = nc.scalar.activation(zT[:, 4 + g, :], pO[:, g * P:(g + 1) * P], ACT.Copy,
                                                scale=pscale[:, g:g + 1])
                last.then_inc(zT_ready, 1)

            def head(v, i):
                c = v % CHUNKS
                keys = (c + 1) * P
                n = HEADS * v + i
                act.wait_ge(maxed, n + 1)
                if i >= 2:
                    act.wait_ge(t_done, batch(v, "p", i - 2) + 1)
                nc.scalar.activation(pr[:, i % 2, 0:keys], sc[:, i % 2, 0:keys], ACT.Exp, bias=att[:, 1, i:i + 1],
                                     accum_out=att[:, 2, i:i + 1]).then_inc(expd, 1)
                b = batch(v, "p", i)
                act.wait_ge(t_done, b + 1)
                if i >= 2:
                    act.wait_ge(pv_done, n - 1)
                nc.scalar.activation(prT[:, i % 2, 0:c + 1, :],
                                     pT[b % 2][:, 0:keys].rearrange("p (k t) -> p k t", t=P),
                                     ACT.Copy).then_inc(t_copied, 1)

            def attout(v, _):
                b = batch(v, "o")
                act.wait_ge(t_done, b + 1)
                nc.scalar.activation(zT[:, 0:4, :], pT[b % 2][:, :].rearrange("p (k t) -> p k t", t=P),
                                     ACT.Copy).then_inc(t_copied, 1)

            def wqread(v, i):
                t = number["wq", v, i]
                n = WQ_TILES * v + i
                wait_product(act, "wq", v, i)
                if i == 0:
                    act.wait_ge(x_mixed, OUT_TILES * v + OUT_TILES)
                nc.scalar.activation(qtok, pG[t % 2][:, :], ACT.Copy).then_inc(g_read[t % 2], 1)
                b = batch(v, "wq", i)
                act.wait_ge(t_done, b + 1)
                nc.scalar.activation(qhT, pT[b % 2][:, :].rearrange("p (k t) -> p k t", t=P),
                                     ACT.Copy).then_inc(t_copied, 1)
                act.wait_ge(keyed, n + 1)
                nc.scalar.activation(S[:, HPT * i:HPT * i + HPT, :, :],
                                     pS[:, :].rearrange("p (h s n) -> p h s n", h=HPT, s=2), ACT.Copy).then_inc(S_in, 1)

            def pick(v, q):
                act.wait_ge(masked, WQ_TILES * v + q + 1)
                gat = gates[:, v % 2, q * HPT * PK:(q + 1) * HPT * PK]
                nc.scalar.activation(gat, gat, ACT.Exp).then_inc(gexp, 1)

            def gather(v, g):
                n = v * GG + g
                act.wait_ge(dotted, n + 1)
                nc.scalar.activation(gel[:, n % 2, :], dots[:, n % 2, :], ACT.Gelu).then_inc(gelued, 1)

            stages = {"modpart": modpart, "mod": mod_, "norm": norm, "inread": inread, "qknorm": qknorm,
                      "pool": pool_, "head": head, "attout": attout, "wqread": wqread, "pick": pick, "gather": gather}
            for name, v, i in order:
                if name in stages:
                    stages[name](v, i)

        @block.vector
        def _(dve):
            steps = [0]

            def link(ins):
                steps[0] += 1
                ins.then_inc(chain, 1)
                dve.wait_ge(chain, steps[0])

            dve.wait_ge(silu_step, 1)
            nc.vector.tensor_scalar(silu[:, 1, :], silu[:, 0, :], 1.0, None, ALU.add).then_inc(silu_step, 1)
            dve.wait_ge(silu_step, 2)
            nc.vector.reciprocal(silu[:, 1, :], silu[:, 1, :]).then_inc(silu_step, 1)
            dve.wait_ge(silu_step, 3)
            nc.vector.tensor_tensor(silu[:, 2, :], cT, silu[:, 1, :], ALU.mult).then_inc(silu_step, 1)

            def rsqrt(y, v_, t):
                link(nc.vector.tensor_scalar(y.bitcast(I32), v_.bitcast(I32), -0.5, float(0x5F3759DF), ALU.mult, ALU.add))
                for _ in range(4):
                    link(nc.vector.tensor_tensor(t, y, y, ALU.mult))
                    link(nc.vector.tensor_tensor(t, t, v_, ALU.mult))
                    link(nc.vector.tensor_scalar(t, t, -0.5, 1.5, ALU.mult, ALU.add))
                    link(nc.vector.tensor_tensor(y, y, t, ALU.mult))

            def mod_(layer, i):
                part, half = divmod(i, 2)
                if part not in GAIN_PARTS:
                    return
                t = number["mod", layer, i]
                dst = mod[:, part, half * NT:(half + 1) * NT]
                dve.wait_ge(gain_in, 32 * (layer + 1))
                dve.wait_ge(mod_done, MOD_TILES * layer + i + 1)
                nc.vector.scalar_tensor_tensor(out=dst, in0=pG[t % 2][:, :], scalar=1.0, in1=dst,
                                               op0=ALU.add, op1=ALU.mult).then_inc(g_read[t % 2], 1)

            def norm(v, which):
                layer, c = divmod(v, CHUNKS)
                if v == 0 and which == 0:
                    dve.wait_ge(consts, CONSTS)
                if which:
                    dve.wait_ge(x_mixed, OUT_TILES * (v + 1))
                for part in ((3, 4) if which else (0, 1)):
                    for half in range(2):
                        wait_read(dve, number["mod", layer, 2 * part + half])
                src = x[:, c, :]
                dst = h2[:, c, :] if which else hm[:, :]
                link(nc.vector.tensor_tensor_reduce(out=dst, in0=src, in1=src, scale=1.0, scalar=0.0,
                                                    op0=ALU.mult, op1=ALU.add, accum_out=ss))
                link(nc.vector.tensor_scalar(ve, ss, 1.0 / D, EPS, ALU.mult, ALU.add))
                rsqrt(rs, ve, r2)
                link(nc.vector.scalar_tensor_tensor(out=dst, in0=src, scalar=rs, in1=mod[:, 4 if which else 1, :],
                                                    op0=ALU.mult, op1=ALU.mult))
                nc.vector.tensor_tensor(dst, dst, mod[:, 3 if which else 0, :], ALU.add).then_inc(h_ready, 1)
                dve.wait_ge(h_ready, 2 * v + which + 1)

            def inread(v, i):
                layer, c = divmod(v, CHUNKS)
                if layer and i % 3 == 1:
                    half = i // 3
                    n = 2 * c + half
                    t = number["in", v, i]
                    wait_product(dve, "in", v, i)
                    wait_read(dve, number["in", v, 3 * half])
                    if n:
                        dve.wait_ge(t_done, batch(v, "ub", 0) + 1 if half else batch(v - 1, "ub", 2) + 1)
                    nc.vector.tensor_tensor(uhalf, pG[t % 2][:, :], xin, ALU.mult).then_inc(g_read[t % 2], 1)

            def qknorm(v, _):
                wait_read(dve, number["in", v, 0])
                wait_read(dve, number["in", v, 1])
                h16 = qk.rearrange("p (h d) -> p h d", d=HD)
                link(nc.vector.tensor_tensor(hm[:, :], qk, qk, ALU.mult))
                link(nc.vector.tensor_reduce(ssq, hm[:, :].rearrange("p (h d) -> p h d", d=HD), axis=AX.X, op=ALU.add))
                link(nc.vector.tensor_scalar(veq, ssq, 1.0 / HD, EPS, ALU.mult, ALU.add))
                rsqrt(rsq, veq, r2q)
                link(nc.vector.tensor_scalar(rsq[:, 0:HEADS], rsq[:, 0:HEADS], HD ** -0.5, None, ALU.mult))
                nc.vector.tensor_tensor(h16, h16, rsq.unsqueeze(2).to_broadcast([P, 2 * HEADS, HD]), ALU.mult)\
                    .then_inc(qk_ready, 1)

            def head(v, i):
                c = v % CHUNKS
                keys = (c + 1) * P
                n = HEADS * v + i

                def masked_max(h):
                    m = HEADS * v + h
                    dve.wait_ge(scored, m + 1)
                    if h == 0:
                        dve.wait_ge(pooled, v + 1)
                    if h >= 2:
                        dve.wait_ge(expd, m - 1)
                    link(nc.vector.tensor_tensor_reduce(
                        out=sc[:, h % 2, 0:keys], in0=score_bank[h % 2][:, 0:keys],
                        in1=bias[:, c * P:c * P + keys], scale=1.0, scalar=LOWEST, op0=ALU.add, op1=ALU.max,
                        accum_out=att[:, 0, h:h + 1]))
                    nc.vector.tensor_scalar(att[:, 1, h:h + 1], att[:, 0, h:h + 1], -1.0, None, ALU.mult)\
                        .then_inc(maxed, 1)

                if i == 0:
                    masked_max(0)
                if i + 1 < HEADS:
                    masked_max(i + 1)

            def attout(v, _):
                dve.wait_ge(expd, HEADS * (v + 1))
                link(nc.vector.reciprocal(att[:, 3, :], att[:, 2, :]))
                dve.wait_ge(pv_done, HEADS * (v + 1))
                nc.vector.tensor_tensor(otok.rearrange("p (h d) -> p h d", d=HD),
                                        pO[:, :].rearrange("p (h d) -> p h d", d=HD),
                                        att[:, 3, :].unsqueeze(2).to_broadcast([P, HEADS, HD]), ALU.mult)\
                    .then_inc(otok_ready, 1)

            def conv(v, _):
                c = v % CHUNKS
                dve.wait_ge(t_copied, batch(v, "ub", 3) + 1)
                if c == 0:
                    link(nc.vector.memset(uT[:, :, 0:2], 0.0))

                def w(lag):
                    return convw[:, lag, :].unsqueeze(2).to_broadcast([P, KC, P])

                link(nc.vector.tensor_tensor(zT, uT[:, :, 2:P + 2], w(0), ALU.mult))
                for lag in (1, 2):
                    link(nc.vector.tensor_tensor(lagT, uT[:, :, 2 - lag:P + 2 - lag], w(lag), ALU.mult))
                    link(nc.vector.tensor_tensor(zT, zT, lagT, ALU.add))
                if c == 0:
                    nc.vector.tensor_copy(uT[:, :, 0:2], uT[:, :, P:P + 2]).then_inc(shifted, 1)
                nc.vector.tensor_tensor(zT, zT, bT, ALU.mult).then_inc(zT_ready, 1)

            def outread(v, i):
                layer, c = divmod(v, CHUNKS)
                t = number["out", v, i]
                wait_product(dve, "out", v, i)
                wait_read(dve, number["mod", layer, 4 + i])
                cols_ = slice(i * NT, (i + 1) * NT)
                if i:
                    dve.wait_ge(x_mixed, OUT_TILES * v + i)
                ins = nc.vector.tensor_tensor(ytmp, pG[t % 2][:, :], mod[:, 2, cols_], ALU.mult)
                ins.then_inc(g_read[t % 2], 1)
                wait_read(dve, t)
                nc.vector.tensor_tensor(x[:, c, cols_], x[:, c, cols_], ytmp, ALU.add).then_inc(x_mixed, 1)

            def top16(values, spare, best, where):
                link(nc.vector.max(best[:, 0:8], values))
                link(nc.vector.max_index(where[:, 0:8], best[:, 0:8], values))
                link(nc.vector.match_replace(spare, best[:, 0:8], values, LOWEST))
                link(nc.vector.max(best[:, 8:16], spare))
                link(nc.vector.max_index(where[:, 8:16], best[:, 8:16], spare))

            def route(v, i):
                h, k = divmod(i, 3)
                if k < 2:
                    dve.wait_ge(S_in, WQ_TILES * v + h // HPT + 1)
                    top16(S[:, h, k, :], s2, v16[:, h, k, :], i16[:, h, k, :])
                    return
                link(nc.vector.tensor_tensor(cand.rearrange("p (a b) -> p a b", a=PK),
                                             v16[:, h, 0, :].unsqueeze(2).to_broadcast([P, PK, PK]),
                                             v16[:, h, 1, :].unsqueeze(1).to_broadcast([P, PK, PK]), ALU.add))
                top16(cand, cand2, vs[:, h, :], ci[:, h, :])

            def heads_gates(v, q):
                return gates[:, v % 2, q * HPT * PK:(q + 1) * HPT * PK].rearrange("p (h k) -> p h k", h=HPT)

            def pick(v, q):
                hs = slice(q * HPT, (q + 1) * HPT)
                nc.vector.tensor_tensor(heads_gates(v, q), vs[:, hs, :], vs[:, hs, 0:1].to_broadcast([P, HPT, PK]),
                                        ALU.subtract).then_inc(masked, 1)
                flat = ci[:, hs, :].rearrange("p h k -> p (h k)")
                link(nc.vector.tensor_single_scalar(cab[:, 0, :], flat, 4, op=ALU.logical_shift_right))
                link(nc.vector.tensor_single_scalar(cab[:, 1, :], flat, PK - 1, op=ALU.bitwise_and))
                hotv = hot.rearrange("p (j a) -> p j a", a=PK)
                hot4 = hot.rearrange("p (h j a) -> p h j a", h=HPT, a=PK)
                n = HPT * PK
                for s in range(2):
                    link(nc.vector.tensor_tensor(hotv, cab[:, s, :].unsqueeze(2).to_broadcast([P, n, PK]),
                                                 iota[:, :].unsqueeze(1).to_broadcast([P, n, PK]), ALU.is_equal))
                    link(nc.vector.tensor_tensor(hot4, hot4, i16[:, hs, s, :].unsqueeze(2)
                                                 .to_broadcast([P, HPT, PK, PK]), ALU.mult))
                    link(nc.vector.tensor_reduce(sub[:, s, :], hotv, axis=AX.X, op=ALU.add))
                nc.vector.scalar_tensor_tensor(out=ids[:, v % 2, q * n:(q + 1) * n], in0=sub[:, 0, :],
                                               scalar=float(NKEY), in1=sub[:, 1, :], op0=ALU.mult, op1=ALU.add)\
                    .then_inc(routed, 1)
                dve.wait_ge(routed, WQ_TILES * v + q + 1)

            def gate(v, q):
                gat = heads_gates(v, q)
                dve.wait_ge(gexp, WQ_TILES * v + q + 1)
                link(nc.vector.tensor_reduce(gsum[:, 0, 0:HPT], gat, axis=AX.X, op=ALU.add))
                link(nc.vector.reciprocal(gsum[:, 1, 0:HPT], gsum[:, 0, 0:HPT]))
                link(nc.vector.tensor_tensor(gat, gat, gsum[:, 1, 0:HPT].unsqueeze(2).to_broadcast([P, HPT, PK]),
                                             ALU.mult))

            def weigh(n):
                v, g = divmod(n, GG)
                dve.wait_ge(gelued, n + 1)
                link(nc.vector.tensor_tensor(coef[:, n % 2, :], gel[:, n % 2, :],
                                             gates[:, v % 2, g * GS:(g + 1) * GS], ALU.mult))
                if n >= 2:
                    dve.wait_ge(summed, GS * (n - 1))
                for s in range(GS):
                    last = nc.vector.tensor_scalar(diag[:, n % 2, s, :], ident[:, :], coef[:, n % 2, s:s + 1],
                                                   None, ALU.mult)
                last.then_inc(diag_ready, 1)

            def gather(v, g):
                n = v * GG + g
                for s in range(GS):
                    j = n * GS + s
                    dve.wait_ge(row_in[j % RING], 16 * (j // RING + 1))
                    last = nc.vector.tensor_tensor_reduce(
                        out=ring[:, j % RING, 0:D], in0=ring[:, j % RING, 0:D], in1=h2[:, v % CHUNKS, :], scale=1.0,
                        scalar=0.0, op0=ALU.mult, op1=ALU.add, accum_out=dots[:, n % 2, s:s + 1])
                last.then_inc(dotted, 1)
                if g:
                    weigh(n - 1)

            def finish(v, _):
                layer, c = divmod(v, CHUNKS)
                weigh(v * GG + GG - 1)
                for half in range(2):
                    wait_read(dve, number["mod", layer, 10 + half])
                dve.wait_ge(summed, SLOTS * (v + 1))
                for half in range(2):
                    cols_ = slice(half * NT, (half + 1) * NT)
                    ins = nc.vector.tensor_tensor(otmp, acc[half][:, :], mod[:, 6 if layer else 5, cols_], ALU.mult)
                    link(ins)
                    ins = nc.vector.tensor_tensor(x[:, c, cols_], x[:, c, cols_], otmp, ALU.add)
                    ins.then_inc(x_summed, 1)
                    dve.wait_ge(x_summed, 2 * v + half + 1)

            stages = {"mod": mod_, "norm": norm, "inread": inread, "qknorm": qknorm, "head": head, "attout": attout,
                      "conv": conv, "outread": outread, "route": route, "pick": pick, "gate": gate,
                      "gather": gather, "finish": finish}
            for name, v, i in order:
                if name in stages:
                    stages[name](v, i)


def shape_constants():
    import numpy as np

    seq = P * CHUNKS
    t = np.arange(seq)
    gap = t[:, None] - t[None, :]
    reach = np.zeros((seq, seq))
    for window, dil in ((128, 1), (512, 4), (2048, 16)):
        reach += (gap >= 0) & (gap % dil == 0) & (gap <= window)
    bias = np.where(reach > 0, np.log(np.maximum(reach, 1)), MASKED).astype(np.float32)
    bias = np.concatenate([bias[:P, :P], bias[P:, :]], axis=1)
    mean = np.zeros((GROUPS, seq, seq))
    for g, w in enumerate(WINDOWS):
        mean[g] = ((gap >= 0) & (gap < w)).T / np.minimum(t + 1, w)[None, :] - np.eye(seq)
    poolm = np.stack([mean[:, :P, :P], mean[:, P:, P:], mean[:, :P, P:]])
    return {
        "ident": np.eye(P, dtype=np.float32),
        "bias": np.ascontiguousarray(bias),
        "poolm": np.ascontiguousarray(poolm.transpose(2, 0, 1, 3).astype(np.float32)),
        "quads": (np.arange(P) % 32 == 0).astype(np.float32)[:, None],
        "iota": np.tile(np.arange(PK, dtype=np.float32), (P, 1)),
    }


def kernel(**inputs):
    import numpy as np
    import concourse.bacc as bacc
    from concourse.bass_utils import run_bass_kernel_spmd

    def columns(a):
        return np.asarray(a).reshape(-1, P).T

    given = {k: np.asarray(v) for k, v in inputs.items()}
    arrays = {k: given[k] for k in ("x", "ada_w", "ada_b", "norm_mix_g", "norm_ffn_g", "ab_w_in", "pool_w",
                                    "ab_w_out", "conv_w_in", "conv_w_out", "peer_w_q")}
    for layer in range(LAYERS):
        arrays[f"uv{layer}"] = np.concatenate([given["peer_u"][layer], given["peer_v"][layer]], axis=1)
    arrays["keyT"] = np.stack([given["peer_key1"], given["peer_key2"]], axis=1).transpose(3, 0, 1, 2)
    arrays["cols"] = np.concatenate([columns(given["c"]), columns(given["ab_q_gain"]), columns(given["ab_k_gain"]),
                                     columns(given["pool_scale"]), columns(given["conv_w"])], axis=1)
    arrays.update(shape_constants())

    nc = bacc.Bacc("TRN2", target_bir_lowering=False, num_devices=1)
    maps, aps = {}, {}
    for name, a in arrays.items():
        maps[f"in_{name}"] = np.ascontiguousarray(a)
        aps[name] = nc.dram_tensor(f"in_{name}", a.shape, mybir.dt.from_np(a.dtype), kind="ExternalInput").ap()
    out = nc.dram_tensor("out_x", given["x"].shape, F32, kind="ExternalOutput").ap()
    trunk(nc, aps, out)
    r = run_bass_kernel_spmd(nc, [maps], core_ids=[0])
    return r.results[0]["out_x"]
```

```python
from contextlib import ExitStack

import concourse.bass as bass
from concourse import mybir
from concourse.alu_op_type import AluOpType as ALU

F32 = mybir.dt.float32
I32 = mybir.dt.int32
U32 = mybir.dt.uint32
ACT = mybir.ActivationFunctionType
AX = mybir.AxisListType

P = 128
D = 1024
KC = D // P
NT = 512
LAYERS = 2
CHUNKS = 2
HEADS, HD = 8, 64
WINDOWS = (2, 4, 8, 16)
GROUPS = len(WINDOWS)
CONV = 3
PH, PK = 8, 16
NKEY = 128
EPS = 1e-6
LOWEST = -3.0e38
MASKED = -1.0e30
SLOTS = PH * PK
SPARE_GROUPS = 3
COST = {"modpart": 2.0, "mod": 1.7, "norm": 6.0, "normT": 2.0, "in": 3.4, "inread": 1.0, "gateT": 2.0, "out": 3.4,
        "outread": 1.3, "wq": 3.4, "wqread": 0.7, "queryT": 0.5, "key": 0.8, "qknorm": 6.0, "qkT": 3.0, "pool": 2.5,
        "poolout": 2.5, "score": 1.5, "probT": 0.0, "value": 0.0, "attout": 1.0, "attT": 1.0, "conv": 8.0,
        "route": 2.3, "pick": 2.5, "gate": 1.0}
RING = 9
GS = 2
GG = SLOTS // GS
WR = 5

MOD_TILES = 6 * D // NT
MIX0_TILES = 4
MIX1_TILES = 6
OUT_TILES = D // NT
WQ_TILES = 2 * PH * P // NT
HPT = PH // WQ_TILES
CONV_ORDER = (0, 4, 2, 1, 5, 3)
GAIN_PARTS = (1, 4)


def mix_tiles(layer):
    return MIX1_TILES if layer else MIX0_TILES


BATCHES = {"normT": 2, "gateT": 2, "qkT": 2, "probT": 1, "attT": 1, "queryT": 1}
SHARED = (WQ_TILES // 2, WQ_TILES)
INPUT_SHARED = (3, 2, 1)
INPUT_ALONE = (0,)


def trunk(nc, a, out):
    def mods(layer, parts):
        tiles = [2 * part + half for part in parts for half in range(2)]
        steps = [("modpart", layer, tiles[0])]
        for this, after in zip(tiles, tiles[1:]):
            steps += [("modpart", layer, after), ("mod", layer, this)]
        return steps + [("mod", layer, tiles[-1])]

    def products(name, v, i):
        return [(name, v, 2 * i), (name, v, 2 * i + 1), (name + "read", v, i)]

    def mixer_input(v, tiles):
        steps = []
        for i in tiles:
            steps += products("in", v, i)
            if v == 0 and i == 1:
                steps.append(("qknorm", v, 0))
            if v >= CHUNKS and i % 3 == 2:
                steps.append(("gateT", v, i // 3))
        return steps

    def mixer1(v):
        steps = [("norm", v, 0), ("normT", v, 0)] + mixer_input(v, range(MIX1_TILES)) + [("conv", v, 0)]
        return steps + projection(v) + [("norm", v, 1), ("normT", v, 1)]

    def attention(v):
        steps = [("qkT", v, 0), ("pool", v, 0), ("poolout", v, 0)]
        for i in range(HEADS + 2):
            steps += [("score", v, i)] if i < HEADS else []
            steps += [("probT", v, i - 1)] if 0 <= i - 1 < HEADS else []
            steps += [("value", v, i - 2)] if i >= 2 else []
        return steps + [("attout", v, 0), ("attT", v, 0)]

    def projection(v):
        return [s for i in range(OUT_TILES) for s in products("out", v, i)]

    def query(v, i):
        return products("wq", v, i) + [("queryT", v, i), ("key", v, i)]

    def routing(v, i):
        heads = range(HPT * i, HPT * i + HPT)
        steps = [[("route", v, 3 * h + k) for k in range(3)] + [("pick", v, h), ("gate", v, h)] for h in heads]
        return sum(steps, [])

    def experts(tiles):
        steps = query(*tiles[0])
        for n, tile in enumerate(tiles):
            steps += spread(routing(*tile), query(*tiles[n + 1]) if n + 1 < len(tiles) else [])
        return steps

    def together(v):
        return [(u, i) for i in range(*SHARED) for u in (v, v + 1)] + [(v + 1, i) for i in range(SHARED[0])]

    def spread(stages, other, step=1):
        steps = [[s] for s in stages]
        for n, s in enumerate(other):
            if n * step < len(steps):
                steps[n * step].append(s)
            else:
                steps.append([s])
        return [s for group in steps for s in group]

    def woven(v, other):
        steps, total, spent, at = [], sum(COST[s[0]] for s in other), 0.0, 0
        for g in range(GG):
            steps.append(("gather", v, g))
            if g == 0 and v:
                steps.append(("finish", v - 1, 0))
            while at < len(other) and spent <= total * (g + 1) / (GG - SPARE_GROUPS):
                spent += COST[other[at][0]]
                steps.append(other[at])
                at += 1
        return steps

    order = mods(0, (0, 1)) + [("norm", 0, 0), ("normT", 0, 0), ("norm", 1, 0)] + mixer_input(0, (0, 1))
    order += [("normT", 1, 0)] + mixer_input(0, (2, 3))
    order += spread(attention(0), mods(0, (2, 3, 4)), 3) + projection(0)
    gate2 = mods(0, (5,))
    order += [("norm", 0, 1)] + gate2[:2] + [("normT", 0, 1)] + query(0, 0)
    order += spread(routing(0, 0), gate2[2:] + query(0, 1) + mixer_input(1, INPUT_SHARED))
    order += woven(0, routing(0, 1) + mixer_input(1, INPUT_ALONE) + [("qknorm", 1, 0)] + attention(1) + projection(1)
                   + [("norm", 1, 1), ("normT", 1, 1)] + experts(together(0)))
    order += woven(1, mods(1, range(6)) + mixer1(2) + experts([(2, i) for i in range(SHARED[0])]))
    order += woven(2, mixer1(3) + experts(together(2)))
    order += woven(3, []) + [("finish", 3, 0)]

    order_ahead, held = [], []
    for stage in order:
        if stage[0] == "gather" and stage[2] >= 2:
            order_ahead += [stage] + held
            held = []
        elif stage[0] in ("gather", "finish"):
            order_ahead += held + [stage]
            held = []
        else:
            held.append(stage)
    order_ahead += held

    number, load, used, source, banked = {}, {}, {}, [], {}
    for name, v, i in order:
        if name in ("modpart", "mod"):
            key = (name, v, i)
        elif name in ("in", "out", "wq") and i % 2 == 0:
            key = (name, v, i // 2)
        else:
            if name == "score" and i == 0:
                banked[v] = [len(number) - 2, len(number) - 1]
            continue
        number[key] = len(number)
        if name == "mod":
            continue
        used[key] = len(load)
        if (name == "wq" and v % CHUNKS and i // 2 in range(*SHARED)
                or name == "in" and v == 1 and i // 2 in INPUT_SHARED):
            load[key] = load[name, v - 1, i // 2]
            continue
        load[key] = len(source)
        layer = v if name == "modpart" else v // CHUNKS
        source.append({
            "modpart": lambda: (a["ada_w"][layer], i),
            "in": lambda: (a["conv_w_in"][0], CONV_ORDER[i // 2]) if layer else (a["ab_w_in"][0], i // 2),
            "out": lambda: ((a["conv_w_out"] if layer else a["ab_w_out"])[0], i // 2),
            "wq": lambda: (a["peer_w_q"][layer], i // 2),
        }[name]())

    through = [2 * max(used[key] for key in load if load[key] == t) + 2 for t in range(len(source))]
    nth, first_batch, counts, batches = {}, {}, {}, 0
    for stage in order:
        nth[stage] = counts[stage[0]] = counts.get(stage[0], -1) + 1
        if stage[0] in BATCHES:
            first_batch[stage] = batches
            batches += BATCHES[stage[0]]

    def batch(name, v, i, k=0):
        return first_batch[name, v, i] + k

    def earlier(name, *stage):
        return sum(s[0] == name for s in order[:order.index(stage)])

    head_order = [[i for name, u, i in order if name == "pick" and u == v] for v in range(LAYERS * CHUNKS)]

    def last_use(n):
        return through[n // 2] - 1 + n % 2

    EARLY = 2 * (load["wq", 0, 0] + 1)
    place, landed, before, tenants = [], [], [], [[] for _ in range(WR + RING)]
    for n in range(2 * len(source)):
        places = range(WR + RING if n < EARLY else WR)
        p = min(places, key=lambda p: last_use(tenants[p][-1]) if tenants[p] else 0)
        before.append(tenants[p][-1] if tenants[p] else None)
        tenants[p].append(n)
        place.append(p)
        landed.append(16 * len(tenants[p]))

    ctx = ExitStack()
    with ctx:
        def sb(name, shape, dt=F32):
            return ctx.enter_context(nc.sbuf_tensor("t_" + name, shape, dt))

        def pb(name, shape):
            return ctx.enter_context(nc.psum_tensor("p_" + name, shape, F32))

        def sem(name):
            return ctx.enter_context(nc.semaphore("s_" + name))

        ring = sb("ring", [P, RING, 2 * D])
        wring = sb("wring", [P, WR, KC // 2, NT])
        x = sb("x", [P, CHUNKS, D])
        mod = sb("mod", [P, 7, D])
        h2 = sb("h2", [P, CHUNKS, D])
        hTs = sb("hT", [P, CHUNKS, KC, P])
        hm = sb("hm", [P, D])

        def normed(v):
            return h2[:, 1, :] if v == 1 else hm[:, :]

        zT = hm[:, :].rearrange("p (k t) -> p k t", k=KC)
        ident = sb("ident", [P, P])
        bias = sb("bias", [P, 3 * P])
        poolm = sb("poolm", [P, 3, GROUPS, P])
        poolw = sb("poolw", [P, GROUPS, P])
        keyT = sb("keyT", [P, LAYERS, 2, P])
        cols = sb("cols", [P, KC + 3 * 4 + CONV * KC])
        cT = cols[:, 0:8]
        qgain, kgain, pscale = cols[:, 8:12], cols[:, 12:16], cols[:, 16:20]
        convw = cols[:, 20:44].rearrange("p (l k) -> p l k", l=CONV)
        iota = sb("iota", [P, PK])
        silu = sb("silu", [P, 2, KC])
        silu32 = sb("silu32", [P, KC, 32])
        ones = sb("ones", [P, 1])
        adab = sb("adab", [P, NT])
        modsum = sb("modsum", [P, 2, NT])

        keep = sb("keep", [P, 3104])
        kT = keep[:, 0:1024].rearrange("p (j t) -> p j t", j=4)
        vtok = keep[:, 1024:2048].rearrange("p (c n) -> p c n", c=CHUNKS)
        utok = keep[:, 2048:3072].rearrange("p (c n) -> p c n", c=CHUNKS)
        uT = keep[:, 0:1040].rearrange("p (k t) -> p k t", k=KC)
        bT = keep[:, 1040:2064].rearrange("p (k t) -> p k t", k=KC)
        lagT = keep[:, 2064:3088].rearrange("p (k t) -> p k t", k=KC)
        work = sb("work", [P, 3072])

        def qk(v):
            return h2[:, 1, :] if v == 1 else work[:, 0:1024]

        otok = work[:, 0:512]
        qT = work[:, 1024:1536].rearrange("p (j t) -> p j t", j=4)
        sc = work[:, 1536:2048].rearrange("p (b t) -> p b t", b=2)
        dT = work[:, 1536:2048].rearrange("p (g t) -> p g t", g=GROUPS)
        pr = work[:, 2048:2560].rearrange("p (b t) -> p b t", b=2)
        prT = work[:, 2560:3072].rearrange("p (b k t) -> p b k t", b=2, k=2)
        xin, uhalf, bhalf = work[:, 0:512], work[:, 512:1024], work[:, 1024:1536]
        ytmp = work[:, 2048:2560]
        S = work[:, 0:2048].rearrange("p (q h s n) -> p q h s n", q=WQ_TILES, h=HPT, s=2)
        qtok = work[:, 2048:2560]
        qhT = work[:, 2560:3072].rearrange("p (j t) -> p j t", j=4)
        cand, cand2 = hm[:, 0:256], hm[:, 256:512]
        s2 = hm[:, 256:384]
        hot = hm[:, 512:1024].rearrange("p (s j a) -> p s j a", s=2, a=PK)

        v16 = sb("v16", [P, 2, PK])
        i16 = sb("i16", [P, 2, PK], U32)
        vs = sb("vs", [P, PK])[:, :]
        ci = sb("ci", [P, PK], U32)[:, :]
        cab = sb("cab", [P, 2, PK], U32)
        sub = sb("sub", [P, 2, PK])
        ids = sb("ids", [P, 2, SLOTS], U32)
        gates = sb("gates", [P, 2, SLOTS])
        small = sb("small", [P, 96])
        ss, ve, rs, r2 = small[:, 0:1], small[:, 1:2], small[:, 2:3], small[:, 3:4]
        ssq, veq, rsq, r2q = small[:, 16:32], small[:, 32:48], small[:, 48:64], small[:, 64:80]
        att = sb("att", [P, 4, HEADS])
        gsum = sb("gsum", [P, 2])
        dots = sb("dots", [P, 2, GS])
        gel = sb("gel", [P, 2, GS])
        coef = sb("coef", [P, 2, GS])
        diag = sb("diag", [P, 2, GS, P])
        otmp = modsum[:, 0, :]

        acc = [pb(f"acc{i}", [P, NT]) for i in range(2)]
        pG = [pb(f"g{i}", [P, NT]) for i in range(2)]
        pT = [pb(f"t{i}", [P, NT]) for i in range(2)]
        pS = pb("s", [P, NT])
        pO = pb("o", [P, NT])
        score_banks = ((pS, acc[0]), (pS, pG[1]))

        cols_in = sem("cols_in")
        mod_consts = sem("mod_consts")
        x_in = sem("x_in")
        mix_consts = sem("mix_consts")
        key_consts = sem("key_consts")
        w_in = [sem(f"w_in{i}") for i in range(WR + RING)]
        halves_done = sem("halves_done")

        t_done = sem("t_done")
        g_read = [sem(f"g_read{i}") for i in range(2)]
        t_copied = sem("t_copied")
        gain_in = sem("gain_in")
        mod_done = sem("mod_done")
        zeroed = sem("zeroed")
        silu_step = sem("silu_step")
        chain = sem("chain")
        h_ready = sem("h_ready")
        qk_ready = sem("qk_ready")
        scored = sem("scored")
        maxed = sem("maxed")
        masked = sem("masked")
        expd = sem("expd")
        pv_done = sem("pv_done")
        otok_ready = sem("otok_ready")
        diff_done = sem("diff_done")
        dT_ready = sem("dT_ready")
        pooled = sem("pooled")
        zT_ready = sem("zT_ready")
        x_mixed = sem("x_mixed")
        keyed = sem("keyed")
        S_in = sem("S_in")
        shifted = sem("shifted")
        gexp = sem("gexp")
        routed = sem("routed")
        row_in = [sem(f"row_in{i}") for i in range(RING)]
        dotted = sem("dotted")
        gelued = sem("gelued")
        diag_ready = sem("diag_ready")
        summed = sem("summed")
        half_summed = sem("half_summed")
        x_summed = sem("x_summed")
        stored = sem("stored")

        def weights_at(n):
            if place[n] < WR:
                return wring[:, place[n], :, :]
            return ring[:, place[n] - WR, :].rearrange("p (k n) -> p k n", n=NT)

        def wait_product(engine, *key):
            engine.wait_ge(halves_done, 2 * used[key] + 2)

        def wait_weights(engine, n):
            engine.wait_ge(halves_done, last_use(n))

        def wait_read(engine, t):
            engine.wait_ge(g_read[t % 2], t // 2 + 1)

        block = ctx.enter_context(nc.Block())

        @block.sync
        def _(sp):
            sp.dma_start(cols[:, :], a["cols"]).then_inc(cols_in, 16)

            def load_weights(t):
                w, i = source[t]
                for half in range(2):
                    n = 2 * t + half
                    if before[n] is not None:
                        wait_weights(sp, before[n])
                    rows = w[half * D // 2:(half + 1) * D // 2, i * NT:(i + 1) * NT]
                    sp.dma_start(weights_at(n), rows.rearrange("(k p) n -> p k n", p=P)).then_inc(w_in[place[n]], 16)

            early = 1
            load_weights(0)
            sp.dma_start(ident[:, :], a["ident"]).then_inc(mod_consts, 16)
            sp.wait_ge(zeroed, 1)
            sp.dma_start(adab[0:LAYERS * MOD_TILES, :], a["ada_b"].rearrange("l (i n) -> (l i) n", n=NT))\
                .then_inc(mod_consts, 16)
            for t in range(early, 3):
                load_weights(t)
            for part in GAIN_PARTS:
                gain = a["norm_mix_g" if part == 1 else "norm_ffn_g"][0, :]
                sp.dma_start(mod[:, part, :], gain.unsqueeze(0).to_broadcast([P, D])).then_inc(gain_in, 16)
            sp.dma_start(x[:, :, :], a["x"][0].rearrange("(c p) d -> p c d", p=P)).then_inc(x_in, 16)
            early = load["in", 0, 3] + 1
            for t in range(3, early):
                load_weights(t)
            sp.dma_start(poolm[:, :, :, :], a["poolm"]).then_inc(mix_consts, 16)
            sp.dma_start(poolw[:, :, :], a["pool_w"][0].rearrange("g c d -> c g d")).then_inc(mix_consts, 16)
            sp.dma_start(bias[:, :], a["bias"]).then_inc(mix_consts, 16)
            sp.dma_start(keyT[:, :, :, :], a["keyT"]).then_inc(key_consts, 16)
            sp.dma_start(iota[:, :], a["iota"]).then_inc(key_consts, 16)
            for t in range(early, len(source)):
                load_weights(t)
            for n in range(2 * CHUNKS):
                c, half = divmod(n, 2)
                sp.wait_ge(x_summed, 2 * CHUNKS + n + 1)
                columns_ = slice(half * NT, (half + 1) * NT)
                sp.dma_start(out[0, c * P:(c + 1) * P, columns_], x[:, c, columns_]).then_inc(stored, 16)
            sp.wait_ge(stored, 16 * 2 * CHUNKS)

        @block.gpsimd
        def _(pool):
            for v in range(LAYERS * CHUNKS):
                layer = v // CHUNKS
                for j in range(SLOTS):
                    if j % PK == 0:
                        h = head_order[v][j // PK]
                        pool.wait_ge(routed, nth["pick", v, h] + 1)
                    n = v * SLOTS + j
                    if n < RING:
                        if tenants[WR + n]:
                            wait_weights(pool, tenants[WR + n][-1])
                    else:
                        pool.wait_ge(summed, n - RING + 1)
                    nc.gpsimd.indirect_dma_start(
                        out=ring[:, n % RING, :], out_offset=None, in_=a[f"uv{layer}"],
                        in_offset=bass.IndirectOffsetOnAxis(ap=ids[:, v % 2, j:j + 1], axis=0),
                    ).then_inc(row_in[n % RING], 16)

        @block.tensor
        def _(pe):
            def free_bank(t):
                if t >= 2:
                    wait_read(pe, t - 2)
                return pG[t % 2]

            def product(key, half, lhsT):
                t, n = number[key], 2 * load[key] + half
                bank = free_bank(t) if half == 0 else pG[t % 2]
                pe.wait_ge(w_in[place[n]], landed[n])
                for k in range(KC // 2):
                    kk = half * KC // 2 + k
                    last = nc.tensor.matmul(bank[:, :], lhsT[:, kk, :], weights_at(n)[:, k, :],
                                            start=kk == 0, stop=kk == KC - 1)
                last.then_inc(halves_done, 1)

            def transposes(b, blocks):
                if b >= 2:
                    pe.wait_ge(t_copied, b - 1)
                for i, block_ in enumerate(blocks):
                    last = nc.tensor.transpose(pT[b % 2][:, i * P:(i + 1) * P], block_, ident[:, :])
                last.then_inc(t_done, 1)

            def modpart(layer, i):
                if i == 0 and layer == 0:
                    pe.wait_ge(silu_step, 4)
                key = ("modpart", layer, i)
                t = number[key]
                bank = free_bank(t)
                for half in range(2):
                    n = 2 * load[key] + half
                    pe.wait_ge(w_in[place[n]], landed[n])
                    for q in range(4):
                        k = 4 * half + q
                        last = nc.tensor.matmul(bank[32 * q:32 * q + 32, :], silu32[:, k, :],
                                                weights_at(n)[:, q, :], start=half == 0, stop=half == 1,
                                                tile_position=(0, 32 * q))
                    last.then_inc(halves_done, 1)

            def mod_(layer, i):
                t = number["mod", layer, i]
                bank = free_bank(t)
                wait_read(pe, number["modpart", layer, i])
                nc.tensor.matmul(bank[:, :], ones[:, 0:1].to_broadcast([P, P]), modsum[:, i % 2, :],
                                 start=True, stop=True).then_inc(mod_done, 1)

            def normT(v, which):
                c = v % CHUNKS
                if v == 0:
                    pe.wait_ge(mod_consts, 32)
                src = h2[:, c, :] if which else normed(v)
                for i in range(2):
                    pe.wait_ge(h_ready, 2 * nth["norm", v, which] + i + 1)
                    transposes(batch("normT", v, which, i),
                               [src[:, (4 * i + j) * P:(4 * i + j + 1) * P] for j in range(4)])

            def in_(v, i):
                if i == 0:
                    pe.wait_ge(t_copied, batch("normT", v, 0, 1) + 1)
                product(("in", v, i // 2), i % 2, hTs[:, v % CHUNKS, :, :])

            def gateT(v, half):
                wait_read(pe, number["in", v, 3 * half + 1])
                transposes(batch("gateT", v, half), [uhalf[:, j * P:(j + 1) * P] for j in range(4)])
                wait_read(pe, number["in", v, 3 * half + 2])
                transposes(batch("gateT", v, half, 1), [bhalf[:, j * P:(j + 1) * P] for j in range(4)])

            def qkT(v, _):
                pe.wait_ge(qk_ready, v + 1)
                for i in range(2):
                    transposes(batch("qkT", v, 0, i), [qk(v)[:, (4 * i + j) * P:(4 * i + j + 1) * P] for j in range(4)])

            def pool_(v, _):
                c = v % CHUNKS
                wait_read(pe, number["in", v, 3])
                if v:
                    pe.wait_ge(S_in, earlier("key", "pool", v, 0))
                else:
                    pe.wait_ge(mix_consts, 48)
                for g in range(GROUPS):
                    for s in range(c + 1):
                        which = (0 if c == 0 else 2 if s == 0 else 1)
                        last = nc.tensor.matmul(pS[:, g * P:(g + 1) * P], utok[:, s, g * P:(g + 1) * P],
                                                poolm[:, which, g, :], start=s == 0, stop=s == c)
                last.then_inc(diff_done, 1)

            def poolout(v, _):
                pe.wait_ge(dT_ready, v + 1)
                for g in range(GROUPS):
                    last = nc.tensor.matmul(pO[:, g * P:(g + 1) * P], poolw[:, g, :], dT[:, g, :],
                                            start=True, stop=True)
                last.then_inc(pooled, 1)

            def score(v, h):
                n = HEADS * v + h
                if h == 0:
                    pe.wait_ge(t_copied, batch("qkT", v, 0, 1) + 1)
                    if v:
                        for t in banked[v]:
                            wait_read(pe, t)
                    pe.wait_ge(dT_ready, v + 1)
                else:
                    pe.wait_ge(scored, n)
                if h >= 2:
                    pe.wait_ge(maxed, n - 1)
                keys = (v % CHUNKS + 1) * P
                rows = slice(HD * (h % 2), HD * (h % 2) + HD)
                nc.tensor.matmul(score_banks[v][h % 2][:, 0:keys], qT[rows, h // 2, :],
                                 kT[rows, h // 2, 0:keys], start=True, stop=True).then_inc(scored, 1)

            def probT(v, h):
                pe.wait_ge(expd, HEADS * v + h + 1)
                transposes(batch("probT", v, h), [pr[:, h % 2, k * P:(k + 1) * P] for k in range(v % CHUNKS + 1)])

            def value(v, h):
                c = v % CHUNKS
                pe.wait_ge(t_copied, batch("probT", v, h) + 1)
                if h == 0:
                    pe.wait_ge(zT_ready, v + 1)
                for k in range(c + 1):
                    last = nc.tensor.matmul(pO[:, h * HD:(h + 1) * HD], prT[:, h % 2, k, :],
                                            vtok[:, k, h * HD:(h + 1) * HD], start=k == 0, stop=k == c)
                last.then_inc(pv_done, 1)

            def attT(v, _):
                pe.wait_ge(otok_ready, v + 1)
                transposes(batch("attT", v, 0), [otok[:, j * P:(j + 1) * P] for j in range(4)])

            def out_(v, i):
                if i == 0:
                    pe.wait_ge(zT_ready, v + 1)
                    if v < CHUNKS:
                        pe.wait_ge(t_copied, batch("attT", v, 0) + 1)
                product(("out", v, i // 2), i % 2, zT)

            def wq(v, i):
                if i % 2 == 0:
                    pe.wait_ge(t_copied, batch("normT", v, 1, 1) + 1)
                product(("wq", v, i // 2), i % 2, hTs[:, v % CHUNKS, :, :])

            def queryT(v, i):
                wait_read(pe, number["wq", v, i])
                transposes(batch("queryT", v, i), [qtok[:, j * P:(j + 1) * P] for j in range(4)])

            def key(v, i):
                layer = v // CHUNKS
                n = nth["key", v, i]
                pe.wait_ge(t_copied, batch("queryT", v, i) + 1)
                if n:
                    pe.wait_ge(S_in, n)
                else:
                    pe.wait_ge(key_consts, 32)
                for j in range(4):
                    last = nc.tensor.matmul(pS[:, j * P:(j + 1) * P], qhT[:, j, :], keyT[:, layer, j % 2, :],
                                            start=True, stop=True)
                last.then_inc(keyed, 1)

            def add_values(n):
                v, g = divmod(n, GG)
                pe.wait_ge(diag_ready, n + 1)
                if g == 0 and v:
                    pe.wait_ge(x_summed, 2 * v)
                slots = [(s, half) for s in range(GS) for half in range(2)]
                if g == GG - 1:
                    slots.sort(key=lambda at: at[1])
                for s, half in slots:
                    j = n * GS + s
                    last = nc.tensor.matmul(acc[half][:, :], diag[:, n % 2, s, :],
                                            ring[:, j % RING, D + half * NT:D + (half + 1) * NT],
                                            start=g == 0 and s == 0, stop=g == GG - 1 and s == GS - 1)
                    if half:
                        last.then_inc(summed, 1)
                    elif g == GG - 1 and s == GS - 1:
                        last.then_inc(half_summed, 1)

            def gather(v, g):
                if g:
                    add_values(v * GG + g - 1)

            def finish(v, _):
                add_values(v * GG + GG - 1)

            stages = {"modpart": modpart, "mod": mod_, "normT": normT, "in": in_, "gateT": gateT, "qkT": qkT,
                      "pool": pool_, "poolout": poolout, "score": score, "probT": probT, "value": value,
                      "attT": attT, "out": out_, "wq": wq, "queryT": queryT, "key": key,
                      "gather": gather, "finish": finish}
            for name, v, i in order:
                if name in stages:
                    stages[name](v, i)

        @block.scalar
        def _(act):
            act.wait_ge(cols_in, 16)
            nc.scalar.activation(silu[:, 0, :], cT, ACT.Exp, scale=-1.0).then_inc(silu_step, 1)

            def modpart(layer, i):
                if layer and i == 0:
                    act.wait_ge(h_ready, 4 * CHUNKS)
                    for part in GAIN_PARTS:
                        gain = a["norm_mix_g" if part == 1 else "norm_ffn_g"][layer, :]
                        act.dma_start(mod[:, part, :], gain.unsqueeze(0).to_broadcast([P, D])).then_inc(gain_in, 16)

            def mod_(layer, i):
                part, half = divmod(i, 2)
                if part in GAIN_PARTS:
                    return
                t = number["mod", layer, i]
                row = 6 if layer and part == 5 else part
                act.wait_ge(mod_done, MOD_TILES * layer + i + 1)
                nc.scalar.activation(mod[:, row, half * NT:(half + 1) * NT], pG[t % 2][:, :], ACT.Copy)\
                    .then_inc(g_read[t % 2], 1)

            def normT(v, which):
                if which:
                    wait_product(act, "in", v, mix_tiles(v // CHUNKS) - 1)
                elif v >= CHUNKS:
                    for i in range(WQ_TILES):
                        wait_product(act, "wq", v - CHUNKS, i)
                for i in range(2):
                    b = batch("normT", v, which, i)
                    act.wait_ge(t_done, b + 1)
                    nc.scalar.activation(hTs[:, v % CHUNKS, 4 * i:4 * i + 4, :],
                                         pT[b % 2][:, :].rearrange("p (k t) -> p k t", t=P),
                                         ACT.Copy).then_inc(t_copied, 1)

            def inread(v, i):
                layer, c = divmod(v, CHUNKS)
                t = number["in", v, i]
                if i == 0 and v >= CHUNKS:
                    act.wait_ge(routed, earlier("pick", "in", v, 0))
                if layer == 0:
                    wait_product(act, "in", v, i)
                    dst = (qk(v)[:, 0:NT], qk(v)[:, NT:2 * NT], vtok[:, c, :], utok[:, c, :])[i]
                    nc.scalar.activation(dst, pG[t % 2][:, :], ACT.Copy).then_inc(g_read[t % 2], 1)
                    return
                half, what = divmod(i, 3)
                n = 2 * c + half
                if what == 0:
                    wait_product(act, "in", v, i)
                    if n:
                        wait_read(act, number["in", v, 1] if half else number["in", v - 1, 4])
                    nc.scalar.activation(xin, pG[t % 2][:, :], ACT.Copy).then_inc(g_read[t % 2], 1)
                elif what == 2:
                    wait_product(act, "in", v, i)
                    if n:
                        act.wait_ge(t_done, batch("gateT", v, 0, 1) + 1 if half else batch("gateT", v - 1, 1, 1) + 1)
                    nc.scalar.activation(bhalf, pG[t % 2][:, :], ACT.Copy).then_inc(g_read[t % 2], 1)

            def gateT(v, half):
                for k, dst in enumerate((uT[:, 4 * half:4 * half + 4, 2:P + 2], bT[:, 4 * half:4 * half + 4, :])):
                    b = batch("gateT", v, half, k)
                    act.wait_ge(t_done, b + 1)
                    if v % CHUNKS and half == 0 and k == 0:
                        act.wait_ge(zT_ready, CHUNKS + 1)
                        act.wait_ge(shifted, 1)
                    nc.scalar.activation(dst, pT[b % 2][:, :].rearrange("p (k t) -> p k t", t=P),
                                         ACT.Copy).then_inc(t_copied, 1)

            def qkT(v, _):
                c = v % CHUNKS
                for i, (gain, dst) in enumerate(((qgain, qT), (kgain, kT[:, :, c * P:(c + 1) * P]))):
                    b = batch("qkT", v, 0, i)
                    act.wait_ge(t_done, b + 1)
                    for j in range(4):
                        last = nc.scalar.activation(dst[:, j, :], pT[b % 2][:, j * P:(j + 1) * P], ACT.Copy,
                                                    scale=gain[:, j:j + 1])
                    last.then_inc(t_copied, 1)

            def pool_(v, _):
                act.wait_ge(diff_done, v + 1)
                nc.scalar.activation(dT, pS[:, :].rearrange("p (g t) -> p g t", g=GROUPS), ACT.Copy)\
                    .then_inc(dT_ready, 1)

            def poolout(v, _):
                act.wait_ge(pooled, v + 1)
                for g in range(GROUPS):
                    last = nc.scalar.activation(zT[:, 4 + g, :], pO[:, g * P:(g + 1) * P], ACT.Copy,
                                                scale=pscale[:, g:g + 1])
                last.then_inc(zT_ready, 1)

            def score(v, h):
                n = HEADS * v + h
                keys = (v % CHUNKS + 1) * P
                act.wait_ge(maxed, n + 1)
                if h >= 2:
                    act.wait_ge(t_done, batch("probT", v, h - 2) + 1)
                nc.scalar.activation(pr[:, h % 2, 0:keys], sc[:, h % 2, 0:keys], ACT.Exp, bias=att[:, 1, h:h + 1],
                                     accum_out=att[:, 2, h:h + 1]).then_inc(expd, 1)

            def probT(v, h):
                c = v % CHUNKS
                b = batch("probT", v, h)
                act.wait_ge(t_done, b + 1)
                if h >= 2:
                    act.wait_ge(pv_done, HEADS * v + h - 1)
                nc.scalar.activation(prT[:, h % 2, 0:c + 1, :],
                                     pT[b % 2][:, 0:(c + 1) * P].rearrange("p (k t) -> p k t", t=P),
                                     ACT.Copy).then_inc(t_copied, 1)

            def attT(v, _):
                b = batch("attT", v, 0)
                act.wait_ge(t_done, b + 1)
                nc.scalar.activation(zT[:, 0:4, :], pT[b % 2][:, :].rearrange("p (k t) -> p k t", t=P),
                                     ACT.Copy).then_inc(t_copied, 1)

            def wqread(v, i):
                t = number["wq", v, i]
                wait_product(act, "wq", v, i)
                act.wait_ge(x_mixed, earlier("outread", "wqread", v, i))
                n = nth["queryT", v, i]
                if n:
                    before = [stage for stage in nth if stage[0] == "queryT" and nth[stage] == n - 1]
                    act.wait_ge(t_done, batch(*before[0]) + 1)
                nc.scalar.activation(qtok, pG[t % 2][:, :], ACT.Copy).then_inc(g_read[t % 2], 1)

            def queryT(v, i):
                b = batch("queryT", v, i)
                act.wait_ge(t_done, b + 1)
                nc.scalar.activation(qhT, pT[b % 2][:, :].rearrange("p (k t) -> p k t", t=P),
                                     ACT.Copy).then_inc(t_copied, 1)

            def key(v, i):
                n = nth["key", v, i]
                act.wait_ge(keyed, n + 1)
                if n >= WQ_TILES:
                    act.wait_ge(routed, HPT * (n - WQ_TILES + 1))
                nc.scalar.activation(S[:, n % WQ_TILES, :, :, :],
                                     pS[:, :].rearrange("p (h s n) -> p h s n", h=HPT, s=2), ACT.Copy).then_inc(S_in, 1)

            def pick(v, h):
                at = head_order[v].index(h) * PK
                act.wait_ge(masked, nth["pick", v, h] + 1)
                gat = gates[:, v % 2, at:at + PK]
                nc.scalar.activation(gat, gat, ACT.Exp).then_inc(gexp, 1)

            def gather(v, g):
                n = v * GG + g
                act.wait_ge(dotted, n + 1)
                nc.scalar.activation(gel[:, n % 2, :], dots[:, n % 2, :], ACT.Gelu).then_inc(gelued, 1)

            stages = {"modpart": modpart, "mod": mod_, "normT": normT, "inread": inread, "gateT": gateT, "qkT": qkT,
                      "pool": pool_, "poolout": poolout, "score": score, "probT": probT, "attT": attT,
                      "wqread": wqread, "queryT": queryT, "key": key, "pick": pick, "gather": gather}
            for name, v, i in order_ahead:
                if name in stages:
                    stages[name](v, i)

        @block.vector
        def _(dve):
            steps = [0]

            def link(ins):
                steps[0] += 1
                ins.then_inc(chain, 1)
                dve.wait_ge(chain, steps[0])

            nc.vector.memset(adab[:, :], 0.0).then_inc(zeroed, 1)
            nc.vector.memset(ones[:, :], 1.0)
            nc.vector.memset(silu32[:, :, :], 0.0).then_inc(zeroed, 1)
            dve.wait_ge(zeroed, 2)
            dve.wait_ge(silu_step, 1)
            nc.vector.tensor_scalar(silu[:, 1, :], silu[:, 0, :], 1.0, None, ALU.add).then_inc(silu_step, 1)
            dve.wait_ge(silu_step, 2)
            nc.vector.reciprocal(silu[:, 1, :], silu[:, 1, :]).then_inc(silu_step, 1)
            dve.wait_ge(silu_step, 3)
            nc.vector.tensor_tensor(silu32[:, :, 31:32], cT.unsqueeze(2), silu[:, 1, :].unsqueeze(2), ALU.mult)\
                .then_inc(silu_step, 1)

            def rsqrt(y, v_, t):
                link(nc.vector.tensor_scalar(y.bitcast(I32), v_.bitcast(I32), -0.5, float(0x5F3759DF),
                                             ALU.mult, ALU.add))
                link(nc.vector.tensor_scalar(v_, v_, -0.5, None, ALU.mult))
                for _ in range(3):
                    if y.shape[-1] == 1:
                        link(nc.vector.scalar_tensor_tensor(out=t, in0=v_, scalar=y, in1=y, op0=ALU.mult, op1=ALU.mult))
                    else:
                        link(nc.vector.tensor_tensor(t, y, y, ALU.mult))
                        link(nc.vector.tensor_tensor(t, t, v_, ALU.mult))
                    link(nc.vector.scalar_tensor_tensor(out=y, in0=t, scalar=1.5, in1=y, op0=ALU.add, op1=ALU.mult))

            def modpart(layer, i):
                t = number["modpart", layer, i]
                n = MOD_TILES * layer + i
                wait_product(dve, "modpart", layer, i)
                if n == 0:
                    dve.wait_ge(mod_consts, 32)
                if n >= 2:
                    dve.wait_ge(mod_done, n - 1)
                nc.vector.scalar_tensor_tensor(out=modsum[:, i % 2, :], in0=adab[:, :], scalar=ident[:, n:n + 1],
                                               in1=pG[t % 2][:, :], op0=ALU.mult, op1=ALU.add)\
                    .then_inc(g_read[t % 2], 1)

            def mod_(layer, i):
                part, half = divmod(i, 2)
                if part not in GAIN_PARTS:
                    return
                t = number["mod", layer, i]
                dst = mod[:, part, half * NT:(half + 1) * NT]
                dve.wait_ge(gain_in, 32 * (layer + 1))
                dve.wait_ge(mod_done, MOD_TILES * layer + i + 1)
                nc.vector.scalar_tensor_tensor(out=dst, in0=pG[t % 2][:, :], scalar=1.0, in1=dst,
                                               op0=ALU.add, op1=ALU.mult).then_inc(g_read[t % 2], 1)

            def norm(v, which):
                layer, c = divmod(v, CHUNKS)
                dve.wait_ge(x_in, 16)
                if which:
                    dve.wait_ge(x_mixed, OUT_TILES * (v + 1))
                src = x[:, c, :]
                dst = h2[:, c, :] if which else normed(v)
                link(nc.vector.tensor_tensor_reduce(out=dst, in0=src, in1=src, scale=1.0, scalar=0.0,
                                                    op0=ALU.mult, op1=ALU.add, accum_out=ss))
                link(nc.vector.tensor_scalar(ve, ss, 1.0 / D, EPS, ALU.mult, ALU.add))
                rsqrt(rs, ve, r2)
                for part in ((3, 4) if which else (0, 1)):
                    for half in range(2):
                        wait_read(dve, number["mod", layer, 2 * part + half])
                n = nth["norm", v, which]
                for half in range(2):
                    cols_ = slice(half * NT, (half + 1) * NT)
                    link(nc.vector.scalar_tensor_tensor(out=dst[:, cols_], in0=src[:, cols_], scalar=rs,
                                                        in1=mod[:, 4 if which else 1, cols_],
                                                        op0=ALU.mult, op1=ALU.mult))
                    nc.vector.tensor_tensor(dst[:, cols_], dst[:, cols_], mod[:, 3 if which else 0, cols_], ALU.add)\
                        .then_inc(h_ready, 1)
                dve.wait_ge(h_ready, 2 * n + 2)

            def inread(v, i):
                layer, c = divmod(v, CHUNKS)
                if layer and i % 3 == 1:
                    half = i // 3
                    n = 2 * c + half
                    t = number["in", v, i]
                    wait_product(dve, "in", v, i)
                    wait_read(dve, number["in", v, 3 * half])
                    if n:
                        dve.wait_ge(t_done, batch("gateT", v, 0, 0) + 1 if half else batch("gateT", v - 1, 1, 0) + 1)
                    nc.vector.tensor_tensor(uhalf, pG[t % 2][:, :], xin, ALU.mult).then_inc(g_read[t % 2], 1)

            def qknorm(v, _):
                wait_read(dve, number["in", v, 0])
                wait_read(dve, number["in", v, 1])
                h16 = qk(v).rearrange("p (h d) -> p h d", d=HD)
                link(nc.vector.tensor_tensor(hm[:, :], qk(v), qk(v), ALU.mult))
                link(nc.vector.tensor_reduce(ssq, hm[:, :].rearrange("p (h d) -> p h d", d=HD), axis=AX.X, op=ALU.add))
                link(nc.vector.tensor_scalar(veq, ssq, 1.0 / HD, EPS, ALU.mult, ALU.add))
                rsqrt(rsq, veq, r2q)
                link(nc.vector.tensor_scalar(rsq[:, 0:HEADS], rsq[:, 0:HEADS], HD ** -0.5, None, ALU.mult))
                nc.vector.tensor_tensor(h16, h16, rsq.unsqueeze(2).to_broadcast([P, 2 * HEADS, HD]), ALU.mult)\
                    .then_inc(qk_ready, 1)

            def score(v, h):
                c = v % CHUNKS
                keys = (c + 1) * P
                n = HEADS * v + h
                dve.wait_ge(scored, n + 1)
                if h == 0:
                    dve.wait_ge(pooled, v + 1)
                    dve.wait_ge(mix_consts, 48)
                if h >= 2:
                    dve.wait_ge(expd, n - 1)
                link(nc.vector.tensor_tensor_reduce(
                    out=sc[:, h % 2, 0:keys], in0=score_banks[v][h % 2][:, 0:keys], in1=bias[:, c * P:c * P + keys],
                    scale=1.0, scalar=LOWEST, op0=ALU.add, op1=ALU.max, accum_out=att[:, 0, h:h + 1]))
                nc.vector.tensor_scalar(att[:, 1, h:h + 1], att[:, 0, h:h + 1], -1.0, None, ALU.mult)\
                    .then_inc(maxed, 1)

            def attout(v, _):
                dve.wait_ge(expd, HEADS * (v + 1))
                link(nc.vector.reciprocal(att[:, 3, :], att[:, 2, :]))
                dve.wait_ge(pv_done, HEADS * (v + 1))
                nc.vector.tensor_tensor(otok.rearrange("p (h d) -> p h d", d=HD),
                                        pO[:, :].rearrange("p (h d) -> p h d", d=HD),
                                        att[:, 3, :].unsqueeze(2).to_broadcast([P, HEADS, HD]), ALU.mult)\
                    .then_inc(otok_ready, 1)

            def conv(v, _):
                c = v % CHUNKS
                dve.wait_ge(t_copied, batch("gateT", v, 1, 1) + 1)
                if c == 0:
                    link(nc.vector.memset(uT[:, :, 0:2], 0.0))

                def w(lag):
                    return convw[:, lag, :].unsqueeze(2).to_broadcast([P, KC, P])

                link(nc.vector.tensor_tensor(zT, uT[:, :, 2:P + 2], w(0), ALU.mult))
                for lag in (1, 2):
                    link(nc.vector.tensor_tensor(lagT, uT[:, :, 2 - lag:P + 2 - lag], w(lag), ALU.mult))
                    link(nc.vector.tensor_tensor(zT, zT, lagT, ALU.add))
                if c == 0:
                    nc.vector.tensor_copy(uT[:, :, 0:2], uT[:, :, P:P + 2]).then_inc(shifted, 1)
                nc.vector.tensor_tensor(zT, zT, bT, ALU.mult).then_inc(zT_ready, 1)

            def outread(v, i):
                layer, c = divmod(v, CHUNKS)
                t = number["out", v, i]
                wait_product(dve, "out", v, i)
                wait_read(dve, number["mod", layer, 4 + i])
                cols_ = slice(i * NT, (i + 1) * NT)
                if i:
                    dve.wait_ge(x_mixed, OUT_TILES * v + i)
                nc.vector.tensor_tensor(ytmp, pG[t % 2][:, :], mod[:, 2, cols_], ALU.mult).then_inc(g_read[t % 2], 1)
                wait_read(dve, t)
                nc.vector.tensor_tensor(x[:, c, cols_], x[:, c, cols_], ytmp, ALU.add).then_inc(x_mixed, 1)

            def top16(values, spare, best, where):
                link(nc.vector.max(best[:, 0:8], values))
                link(nc.vector.max_index(where[:, 0:8], best[:, 0:8], values))
                link(nc.vector.match_replace(spare, best[:, 0:8], values, LOWEST))
                link(nc.vector.max(best[:, 8:16], spare))
                link(nc.vector.max_index(where[:, 8:16], best[:, 8:16], spare))

            def route(v, i):
                h, k = divmod(i, 3)
                if k < 2:
                    tile = nth["key", v, h // HPT]
                    dve.wait_ge(S_in, tile + 1)
                    top16(S[:, tile % WQ_TILES, h % HPT, k, :], s2, v16[:, k, :], i16[:, k, :])
                    return
                link(nc.vector.tensor_tensor(cand.rearrange("p (a b) -> p a b", a=PK),
                                             v16[:, 0, :].unsqueeze(2).to_broadcast([P, PK, PK]),
                                             v16[:, 1, :].unsqueeze(1).to_broadcast([P, PK, PK]), ALU.add))
                top16(cand, cand2, vs, ci)

            def pick(v, h):
                at = head_order[v].index(h) * PK
                here = slice(at, at + PK)
                nc.vector.tensor_tensor(gates[:, v % 2, here], vs, vs[:, 0:1].to_broadcast([P, PK]),
                                        ALU.subtract).then_inc(masked, 1)
                link(nc.vector.tensor_single_scalar(cab[:, 0, :], ci, 4, op=ALU.logical_shift_right))
                link(nc.vector.tensor_single_scalar(cab[:, 1, :], ci, PK - 1, op=ALU.bitwise_and))
                link(nc.vector.tensor_tensor(hot, cab[:, :, :].unsqueeze(3).to_broadcast([P, 2, PK, PK]),
                                             iota[:, :].unsqueeze(1).unsqueeze(1).to_broadcast([P, 2, PK, PK]),
                                             ALU.is_equal))
                link(nc.vector.tensor_tensor(hot, hot, i16[:, :, :].unsqueeze(2).to_broadcast([P, 2, PK, PK]),
                                             ALU.mult))
                link(nc.vector.tensor_reduce(sub[:, :, :], hot, axis=AX.X, op=ALU.add))
                nc.vector.scalar_tensor_tensor(out=ids[:, v % 2, here], in0=sub[:, 0, :], scalar=float(NKEY),
                                               in1=sub[:, 1, :], op0=ALU.mult, op1=ALU.add).then_inc(routed, 1)
                dve.wait_ge(routed, nth["pick", v, h] + 1)

            def gate(v, h):
                at = head_order[v].index(h) * PK
                gat = gates[:, v % 2, at:at + PK]
                dve.wait_ge(gexp, nth["pick", v, h] + 1)
                link(nc.vector.tensor_reduce(gsum[:, 0:1], gat, axis=AX.X, op=ALU.add))
                link(nc.vector.reciprocal(gsum[:, 1:2], gsum[:, 0:1]))
                link(nc.vector.tensor_scalar(gat, gat, gsum[:, 1:2], None, ALU.mult))

            def weigh(n):
                v, g = divmod(n, GG)
                dve.wait_ge(gelued, n + 1)
                link(nc.vector.tensor_tensor(coef[:, n % 2, :], gel[:, n % 2, :],
                                             gates[:, v % 2, g * GS:(g + 1) * GS], ALU.mult))
                if n >= 2:
                    dve.wait_ge(summed, GS * (n - 1))
                for s in range(GS):
                    last = nc.vector.tensor_scalar(diag[:, n % 2, s, :], ident[:, :], coef[:, n % 2, s:s + 1],
                                                   None, ALU.mult)
                last.then_inc(diag_ready, 1)

            def gather(v, g):
                n = v * GG + g
                for s in range(GS):
                    j = n * GS + s
                    dve.wait_ge(row_in[j % RING], 16 * (j // RING + 1))
                    last = nc.vector.tensor_tensor_reduce(
                        out=ring[:, j % RING, 0:D], in0=ring[:, j % RING, 0:D], in1=h2[:, v % CHUNKS, :], scale=1.0,
                        scalar=0.0, op0=ALU.mult, op1=ALU.add, accum_out=dots[:, n % 2, s:s + 1])
                last.then_inc(dotted, 1)
                if g:
                    weigh(n - 1)

            def finish(v, _):
                layer, c = divmod(v, CHUNKS)
                weigh(v * GG + GG - 1)
                for half in range(2):
                    wait_read(dve, number["mod", layer, 10 + half])
                for half in range(2):
                    if half:
                        dve.wait_ge(summed, SLOTS * (v + 1))
                    else:
                        dve.wait_ge(half_summed, v + 1)
                    cols_ = slice(half * NT, (half + 1) * NT)
                    link(nc.vector.tensor_tensor(otmp, acc[half][:, :], mod[:, 6 if layer else 5, cols_], ALU.mult))
                    nc.vector.tensor_tensor(x[:, c, cols_], x[:, c, cols_], otmp, ALU.add).then_inc(x_summed, 1)
                    dve.wait_ge(x_summed, 2 * v + half + 1)

            stages = {"modpart": modpart, "mod": mod_, "norm": norm, "inread": inread, "qknorm": qknorm,
                      "score": score, "attout": attout, "conv": conv, "outread": outread, "route": route, "pick": pick, "gate": gate,
                      "gather": gather, "finish": finish}
            for name, v, i in order_ahead:
                if name in stages:
                    stages[name](v, i)


def shape_constants():
    import numpy as np

    seq = P * CHUNKS
    t = np.arange(seq)
    gap = t[:, None] - t[None, :]
    reach = np.zeros((seq, seq))
    for window, dil in ((128, 1), (512, 4), (2048, 16)):
        reach += (gap >= 0) & (gap % dil == 0) & (gap <= window)
    bias = np.where(reach > 0, np.log(np.maximum(reach, 1)), MASKED).astype(np.float32)
    bias = np.concatenate([bias[:P, :P], bias[P:, :]], axis=1)
    mean = np.zeros((GROUPS, seq, seq))
    for g, w in enumerate(WINDOWS):
        mean[g] = ((gap >= 0) & (gap < w)).T / np.minimum(t + 1, w)[None, :] - np.eye(seq)
    poolm = np.stack([mean[:, :P, :P], mean[:, P:, P:], mean[:, :P, P:]])
    return {
        "ident": np.eye(P, dtype=np.float32),
        "bias": np.ascontiguousarray(bias),
        "poolm": np.ascontiguousarray(poolm.transpose(2, 0, 1, 3).astype(np.float32)),
        "iota": np.tile(np.arange(PK, dtype=np.float32), (P, 1)),
    }


def kernel(**inputs):
    import numpy as np
    import concourse.bacc as bacc
    from concourse.bass_utils import run_bass_kernel_spmd

    def columns(a):
        return np.asarray(a).reshape(-1, P).T

    given = {k: np.asarray(v) for k, v in inputs.items()}
    arrays = {k: given[k] for k in ("x", "ada_w", "ada_b", "norm_mix_g", "norm_ffn_g", "ab_w_in", "pool_w",
                                    "ab_w_out", "conv_w_in", "conv_w_out", "peer_w_q")}
    for layer in range(LAYERS):
        arrays[f"uv{layer}"] = np.concatenate([given["peer_u"][layer], given["peer_v"][layer]], axis=1)
    arrays["keyT"] = np.stack([given["peer_key1"], given["peer_key2"]], axis=1).transpose(3, 0, 1, 2)
    arrays["cols"] = np.concatenate([columns(given["c"]), columns(given["ab_q_gain"]), columns(given["ab_k_gain"]),
                                     columns(given["pool_scale"]), columns(given["conv_w"])], axis=1)
    arrays.update(shape_constants())

    nc = bacc.Bacc("TRN2", target_bir_lowering=False, num_devices=1, dynamic_dma_scratch_size=7168)
    maps, aps = {}, {}
    for name, a in arrays.items():
        maps[f"in_{name}"] = np.ascontiguousarray(a)
        aps[name] = nc.dram_tensor(f"in_{name}", a.shape, mybir.dt.from_np(a.dtype), kind="ExternalInput").ap()
    out = nc.dram_tensor("out_x", given["x"].shape, F32, kind="ExternalOutput").ap()
    trunk(nc, aps, out)
    r = run_bass_kernel_spmd(nc, [maps], core_ids=[0])
    return r.results[0]["out_x"]
```
